# Optimizing a Trainium2 kernel written in Bass

```python
import math
import jax, jax.numpy as jnp
from jax import lax
import numpy as np

D_MODEL = 1024
BATCH = 1
SEQ = 1024
DEPTH = 1

GRID_W = 64
CTX_LEN = 256
MLA_HEADS = 8
MLA_NOPE = 64
MLA_ROPE = 32
MLA_V = 64
Q_LORA = 512
KV_LORA = 256
QBLK = 128
ROPE_BASE = 10000.0
DN_HEADS = 4
DN_DK = 128
DN_DV = 128
DN_QK = DN_HEADS * DN_DK
DN_VW = DN_HEADS * DN_DV
CONV_W = 3
CHUNK = 64
FF_HIDDEN = -(-8 * D_MODEL // (3 * 256)) * 256
EPS = 1e-6
IN_SIZES = (Q_LORA, KV_LORA, MLA_ROPE, 2 * DN_QK + DN_VW, DN_VW, 2 * DN_HEADS, 2 * DN_HEADS, D_MODEL, D_MODEL)
IN_COLS = sum(IN_SIZES)

kernel_name = 'hybrid_mla_gdn_flow_block'

def rmsnorm(x, g):
    xf = x.astype(jnp.float32)
    y = xf * lax.rsqrt(jnp.mean(xf * xf, axis=-1, keepdims=True) + EPS)
    return (y * g.astype(jnp.float32)).astype(x.dtype)

def l2norm(a):
    af = a.astype(jnp.float32)
    return (af * lax.rsqrt(jnp.sum(af * af, axis=-1, keepdims=True) + EPS)).astype(a.dtype)

def modulate(h, shift, scale):
    return h * (1.0 + scale) + shift

def split_cols(p):
    out = []
    start = 0
    for n in IN_SIZES:
        out.append(p[..., start:start + n])
        start += n
    return out

def axial_rope_tables(rows):
    row = jnp.repeat(jnp.arange(rows, dtype=jnp.float32), GRID_W)
    col = jnp.tile(jnp.arange(GRID_W, dtype=jnp.float32), rows)
    n_freq = MLA_ROPE // 4
    inv = ROPE_BASE ** (-jnp.arange(n_freq, dtype=jnp.float32) / n_freq)
    ang = jnp.concatenate([row[:, None] * inv, col[:, None] * inv], axis=-1)
    return jnp.cos(ang), jnp.sin(ang)

def apply_axial_rope(x, cos, sin):
    B, T, Hh, _ = x.shape
    n_freq = MLA_ROPE // 4
    xr = x.reshape(B, T, Hh, 2, 2, n_freq)
    cs = cos.reshape(T, 1, 2, n_freq).astype(x.dtype)
    sn = sin.reshape(T, 1, 2, n_freq).astype(x.dtype)
    x1, x2 = xr[..., 0, :], xr[..., 1, :]
    out = jnp.stack([x1 * cs - x2 * sn, x1 * sn + x2 * cs], axis=-2)
    return out.reshape(B, T, Hh, MLA_ROPE)

def mla_query(cq, g_q_lora, w_uq, cos, sin):
    B, T, _ = cq.shape
    q = (rmsnorm(cq, g_q_lora) @ w_uq).reshape(B, T, MLA_HEADS, MLA_NOPE + MLA_ROPE)
    if cos is None:
        return q
    return jnp.concatenate([q[..., :MLA_NOPE], apply_axial_rope(q[..., MLA_NOPE:], cos, sin)], axis=-1)

def mla_key_value(ckv, kr, g_kv_lora, w_ukv, cos, sin):
    B, T, _ = ckv.shape
    kv = (rmsnorm(ckv, g_kv_lora) @ w_ukv).reshape(B, T, MLA_HEADS, MLA_NOPE + MLA_V)
    k_rope = kr[:, :, None, :]
    if cos is not None:
        k_rope = apply_axial_rope(k_rope, cos, sin)
    k = jnp.concatenate([kv[..., :MLA_NOPE], jnp.broadcast_to(k_rope, (B, T, MLA_HEADS, MLA_ROPE))], axis=-1)
    return k, kv[..., MLA_NOPE:]

def attend(q, k, v):
    B, T, H, Dqk = q.shape
    nb = T // QBLK
    scale = Dqk ** -0.5
    qb = q.reshape(B, nb, QBLK, H, Dqk).swapaxes(0, 1)

    def block(qi):
        s = jnp.einsum('bqhd,bkhd->bhqk', qi, k).astype(jnp.float32) * scale
        p = jax.nn.softmax(s, axis=-1).astype(v.dtype)
        return jnp.einsum('bhqk,bkhd->bqhd', p, v)

    o = lax.map(block, qb)
    return o.swapaxes(0, 1).reshape(B, T, H, v.shape[-1])

def short_conv(u, w):
    T = u.shape[1]
    pad = CONV_W // 2
    up = jnp.pad(u, ((0, 0), (pad, pad), (0, 0)))
    out = up[:, 0:T] * w[0]
    for i in range(1, CONV_W):
        out = out + up[:, i:i + T] * w[i]
    return out

def deltanet_prep(qkv_raw, beta_raw, alpha_raw, conv_w, a_log, dt_bias):
    B, T, _ = qkv_raw.shape
    qkv = jax.nn.silu(short_conv(qkv_raw, conv_w))
    q = l2norm(qkv[..., :DN_QK].reshape(B, T, DN_HEADS, DN_DK))
    k = l2norm(qkv[..., DN_QK:2 * DN_QK].reshape(B, T, DN_HEADS, DN_DK))
    v = qkv[..., 2 * DN_QK:].reshape(B, T, DN_HEADS, DN_DV)
    beta = jax.nn.sigmoid(beta_raw.astype(jnp.float32)).reshape(B, T, 2, DN_HEADS)
    g = -jnp.exp(a_log.astype(jnp.float32)) * jax.nn.softplus(
        alpha_raw.astype(jnp.float32).reshape(B, T, 2, DN_HEADS) + dt_bias.astype(jnp.float32))
    return q, k, v, beta, g

def chunk_gated_delta(q, k, v, g, beta, s0, emit_out):
    out_dtype = v.dtype
    B, T, H, DK = k.shape
    DV = v.shape[-1]
    N = T // CHUNK
    f = jnp.float32

    def chunks(a):
        return a.astype(f).reshape(B, N, CHUNK, H, -1).transpose(1, 0, 3, 2, 4)

    kc, vc = chunks(k), chunks(v)
    gc = jnp.cumsum(chunks(g[..., None])[..., 0], axis=-1)
    bc = chunks(beta[..., None])[..., 0]
    idx = jnp.arange(CHUNK)
    incl = idx[:, None] >= idx[None, :]
    strict = idx[:, None] > idx[None, :]
    decay = jnp.exp(jnp.where(incl, gc[..., :, None] - gc[..., None, :], -jnp.inf))
    kk = jnp.einsum('nbhcd,nbhed->nbhce', kc, kc)
    a_mat = jnp.where(strict, kk * bc[..., :, None] * decay, 0.0) + jnp.eye(CHUNK, dtype=f)
    rhs = jnp.concatenate([vc * bc[..., None], kc * (bc * jnp.exp(gc))[..., None]], axis=-1)
    sol = lax.linalg.triangular_solve(a_mat, rhs, left_side=True, lower=True, unit_diagonal=True)
    u, w = sol[..., :DV], sol[..., DV:]
    if emit_out:
        qc = chunks(q) * DK ** -0.5
        qk = jnp.einsum('nbhcd,nbhed->nbhce', qc, kc) * decay
        xs = (kc, u, w, gc, qc, qk)
    else:
        xs = (kc, u, w, gc)

    def step(S, xs_i):
        k_i, u_i, w_i, g_i = xs_i[:4]
        v_new = u_i - jnp.einsum('bhcd,bhde->bhce', w_i, S)
        g_last = g_i[..., -1]
        S_next = S * jnp.exp(g_last)[..., None, None] + jnp.einsum(
            'bhcd,bhce->bhde', k_i * jnp.exp(g_last[..., None] - g_i)[..., None], v_new)
        if emit_out:
            q_i, qk_i = xs_i[4], xs_i[5]
            o = jnp.einsum('bhcd,bhde->bhce', q_i * jnp.exp(g_i)[..., None], S) + jnp.einsum(
                'bhce,bhef->bhcf', qk_i, v_new)
            return S_next, o
        return S_next, None

    s_final, o = lax.scan(step, s0.astype(f), xs)
    if not emit_out:
        return None, s_final
    o = o.transpose(1, 0, 3, 2, 4).reshape(B, T, H, DV).astype(out_dtype)
    return o, s_final

def flip(a):
    return jnp.flip(a, axis=1)

def gated_rmsnorm(o, z, g):
    B, T = o.shape[:2]
    y = rmsnorm(o, g) * jax.nn.silu(z.reshape(o.shape))
    return y.reshape(B, T, -1)

def merge_branches(o_mla, o_dn, gate_a, gate_b, w_o_mla, w_o_dn, w_out):
    B, T = o_mla.shape[:2]
    y_a = o_mla.reshape(B, T, -1) @ w_o_mla
    y_b = o_dn @ w_o_dn
    return (jax.nn.sigmoid(gate_a) * y_a + jax.nn.sigmoid(gate_b) * y_b) @ w_out

def token_mixer(u, uc, cos, sin, with_ctx_out, w_in, g_q_lora, w_uq, g_kv_lora, w_ukv, w_o_mla,
                conv_qkv, a_log, dt_bias, g_dn_out, w_o_dn, w_out):
    cq, ckv, kr, qkv_raw, z, beta_raw, alpha_raw, gate_a, gate_b = split_cols(u @ w_in)
    cq_c, ckv_c, kr_c, qkv_c, z_c, beta_c, alpha_c, gate_a_c, gate_b_c = split_cols(uc @ w_in)
    q = mla_query(cq, g_q_lora, w_uq, cos, sin)
    k, v = mla_key_value(ckv, kr, g_kv_lora, w_ukv, cos, sin)
    k_c, v_c = mla_key_value(ckv_c, kr_c, g_kv_lora, w_ukv, None, None)
    o_mla = attend(q, jnp.concatenate([k, k_c], axis=1), jnp.concatenate([v, v_c], axis=1))
    ql, kl, vl, bl, gl = deltanet_prep(qkv_raw, beta_raw, alpha_raw, conv_qkv, a_log, dt_bias)
    qx, kx, vx, bx, gx = deltanet_prep(qkv_c, beta_c, alpha_c, conv_qkv, a_log, dt_bias)
    s0 = jnp.zeros((u.shape[0], DN_HEADS, DN_DK, DN_DV), jnp.float32)
    of_c, sf_c = chunk_gated_delta(qx, kx, vx, gx[:, :, 0], bx[:, :, 0], s0, with_ctx_out)
    ob_c, sb_c = chunk_gated_delta(flip(qx), flip(kx), flip(vx), flip(gx[:, :, 1]), flip(bx[:, :, 1]), s0, with_ctx_out)
    of_l, _ = chunk_gated_delta(ql, kl, vl, gl[:, :, 0], bl[:, :, 0], sf_c, True)
    ob_l, _ = chunk_gated_delta(flip(ql), flip(kl), flip(vl), flip(gl[:, :, 1]), flip(bl[:, :, 1]), sb_c, True)
    o_dn = gated_rmsnorm(of_l + flip(ob_l), z, g_dn_out)
    y = merge_branches(o_mla, o_dn, gate_a, gate_b, w_o_mla, w_o_dn, w_out)
    if not with_ctx_out:
        return y, None
    q_c = mla_query(cq_c, g_q_lora, w_uq, None, None)
    o_mla_c = attend(q_c, k_c, v_c)
    o_dn_c = gated_rmsnorm(of_c + flip(ob_c), z_c, g_dn_out)
    y_c = merge_branches(o_mla_c, o_dn_c, gate_a_c, gate_b_c, w_o_mla, w_o_dn, w_out)
    return y, y_c

def swiglu(u, w_in, w_out):
    gu = u @ w_in
    return (jax.nn.silu(gu[..., :FF_HIDDEN]) * gu[..., FF_HIDDEN:]) @ w_out

def setup_inputs(seed: int = 0) -> dict:
    key = jax.random.key(seed)
    ks = jax.random.split(key, 26)
    L = DEPTH
    f = jnp.float32

    def nrm(k, shape, fan_in, s=1.0):
        return jax.random.normal(k, shape, f) * (s * fan_in ** -0.5)

    def gain(k, n):
        return 1.0 + 0.1 * jax.random.normal(k, (L, n), f)

    dt = jnp.exp(jax.random.uniform(ks[20], (L, 2, DN_HEADS), f, minval=math.log(1e-3), maxval=math.log(1e-1)))
    return {
        'x': jax.random.normal(ks[0], (BATCH, SEQ, D_MODEL), f),
        'c': jax.random.normal(ks[1], (BATCH, D_MODEL), f),
        'ctx': jax.random.normal(ks[2], (BATCH, CTX_LEN, D_MODEL), f),
        'c_ctx': jax.random.normal(ks[3], (D_MODEL,), f),
        'w_mod': nrm(ks[4], (L, D_MODEL, 6 * D_MODEL), D_MODEL, 0.5),
        'b_mod': 0.02 * jax.random.normal(ks[5], (L, 6 * D_MODEL), f),
        'g_pre_mix': gain(ks[6], D_MODEL),
        'g_post_mix': gain(ks[7], D_MODEL),
        'g_pre_ffn': gain(ks[8], D_MODEL),
        'g_post_ffn': gain(ks[9], D_MODEL),
        'w_in': nrm(ks[10], (L, D_MODEL, IN_COLS), D_MODEL),
        'g_q_lora': gain(ks[11], Q_LORA),
        'w_uq': nrm(ks[12], (L, Q_LORA, MLA_HEADS * (MLA_NOPE + MLA_ROPE)), Q_LORA),
        'g_kv_lora': gain(ks[13], KV_LORA),
        'w_ukv': nrm(ks[14], (L, KV_LORA, MLA_HEADS * (MLA_NOPE + MLA_V)), KV_LORA),
        'w_o_mla': nrm(ks[15], (L, MLA_HEADS * MLA_V, D_MODEL), MLA_HEADS * MLA_V),
        'conv_qkv': nrm(ks[16], (L, CONV_W, 2 * DN_QK + DN_VW), CONV_W),
        'a_log': jnp.log(jax.random.uniform(ks[17], (L, 2, DN_HEADS), f, minval=1.0, maxval=16.0)),
        'dt_bias': dt + jnp.log(-jnp.expm1(-dt)),
        'g_dn_out': gain(ks[18], DN_DV),
        'w_o_dn': nrm(ks[19], (L, DN_VW, D_MODEL), DN_VW),
        'w_out': nrm(ks[21], (L, D_MODEL, D_MODEL), D_MODEL),
        'w_ffn_in': nrm(ks[22], (L, D_MODEL, 2 * FF_HIDDEN), D_MODEL),
        'w_ffn_out': nrm(ks[23], (L, FF_HIDDEN, D_MODEL), FF_HIDDEN),
    }

def reference(x, c, ctx, c_ctx, w_mod, b_mod, g_pre_mix, g_post_mix, g_pre_ffn, g_post_ffn, w_in,
              g_q_lora, w_uq, g_kv_lora, w_ukv, w_o_mla, conv_qkv, a_log, dt_bias, g_dn_out, w_o_dn,
              w_out, w_ffn_in, w_ffn_out):
    rows = x.shape[1] // GRID_W
    cos, sin = axial_rope_tables(rows)
    h_c = ctx
    for layer in range(DEPTH):
        ctx_out = layer < DEPTH - 1
        mod = jax.nn.silu(c) @ w_mod[layer] + b_mod[layer]
        mod_c = jax.nn.silu(c_ctx) @ w_mod[layer] + b_mod[layer]
        sh1, sc1, gt1, sh2, sc2, gt2 = jnp.split(mod[:, None, :], 6, axis=-1)
        sh1c, sc1c, gt1c, sh2c, sc2c, gt2c = jnp.split(mod_c, 6)
        u = modulate(rmsnorm(x, g_pre_mix[layer]), sh1, sc1)
        uc = modulate(rmsnorm(h_c, g_pre_mix[layer]), sh1c, sc1c)
        y, y_c = token_mixer(u, uc, cos, sin, ctx_out, w_in[layer], g_q_lora[layer], w_uq[layer],
                             g_kv_lora[layer], w_ukv[layer], w_o_mla[layer], conv_qkv[layer], a_log[layer],
                             dt_bias[layer], g_dn_out[layer], w_o_dn[layer], w_out[layer])
        x = x + gt1 * rmsnorm(y, g_post_mix[layer])
        u = modulate(rmsnorm(x, g_pre_ffn[layer]), sh2, sc2)
        x = x + gt2 * rmsnorm(swiglu(u, w_ffn_in[layer], w_ffn_out[layer]), g_post_ffn[layer])
        if ctx_out:
            h_c = h_c + gt1c * rmsnorm(y_c, g_post_mix[layer])
            uc = modulate(rmsnorm(h_c, g_pre_ffn[layer]), sh2c, sc2c)
            h_c = h_c + gt2c * rmsnorm(swiglu(uc, w_ffn_in[layer], w_ffn_out[layer]), g_post_ffn[layer])
    return x


_drawn_inputs = setup_inputs


def setup_inputs(seed=0):
    import zlib

    import numpy as np

    out = dict(_drawn_inputs(seed))
    spreads = {}
    factors = {'ctx': 4.24, 'g_q_lora': 8.0, 'g_kv_lora': 4.738, 'a_log': 3.029}
    for name, (base, spread) in spreads.items():
        noise = np.random.default_rng([zlib.crc32(name.encode()), seed]).standard_normal(out[name].shape)
        drawn = base * np.exp(spread * noise) if base else spread * noise
        out[name] = __import__('jax').numpy.asarray(drawn.astype(out[name].dtype))
    for name, factor in factors.items():
        out[name] = (out[name] * factor).astype(out[name].dtype)
    return out
```

```python
from contextlib import ExitStack

import numpy as np
import concourse.bass as bass
from concourse import mybir

F32 = mybir.dt.float32
F32R = mybir.dt.float32r
ALU = mybir.AluOpType
ACT = mybir.ActivationFunctionType
AX = mybir.AxisListType

P = 128
D = 1024
KD = D // P
T = 1024
TC = 256
TA = T + TC
NT, NC, NA = T // P, TC // P, TA // P
HALF = 512
EPS = 1e-6
CQ, CKV, ROPE = 512, 256, 32
HEADS, NOPE, VD = 8, 64, 64
QKD = NOPE + ROPE
DH, DK = 4, 128
GRID_W, ROPE_BASE = 64, 10000.0
FF = 2816
NFF = FF // P
O_CKV = CQ
O_KR = O_CKV + CKV
O_QKV = O_KR + ROPE
O_Z = O_QKV + 3 * DH * DK
O_BA = O_Z + DH * DK
O_GATE = O_BA + 4 * DH
V_BMOD, V_G1, V_G2, V_GQ, V_GKV, V_CONV, V_GDN, V_ROWS = 16, 64, 72, 80, 84, 86, 122, 123
LEVELS = [1, 2, 4, 8, 16, 32, 64]


def constants():
    i = np.arange(P)
    ident = np.eye(P)
    ones = np.ones((P, P))
    le = (i[:, None] <= i[None, :]) * 1.0
    ge = (i[:, None] >= i[None, :]) * 1.0
    tri = np.concatenate([ident, ones, le, ge, 1 - ge, 1 - le], axis=1)
    lower = []
    for s in LEVELS:
        same = (i[:, None] // (2 * s)) == (i[None, :] // (2 * s))
        lower.append(same & ((i[:, None] // s) % 2 == 1) & ((i[None, :] // s) % 2 == 0))
    levels = np.concatenate([m * 1.0 for m in lower] + [m.T * 1.0 for m in lower], axis=1)
    nf = ROPE // 4
    inv = ROPE_BASE ** (-np.arange(nf, dtype=np.float32) / nf)
    t = np.arange(T)
    ang = np.stack([(t // GRID_W)[:, None] * inv, (t % GRID_W)[:, None] * inv], axis=1)
    cos = np.stack([np.cos(ang), np.cos(ang)], axis=2).reshape(T, ROPE).T
    sin = np.stack([-np.sin(ang), np.sin(ang)], axis=2).reshape(T, ROPE).T
    rope = np.concatenate([cos, sin, cos, sin], axis=0)
    return [np.ascontiguousarray(a, dtype=np.float32) for a in (tri, levels, rope)]


class Own:

    def __init__(self, eng, sem):
        self.eng, self.sem, self.n, self.turn = eng, sem, 0, 0

    def mark(self, ins):
        ins.then_inc(self.sem, 1)
        self.n += 1
        return self.n + self.turn

    def wait(self, value=None):
        self.eng.wait_ge(self.sem, self.n + self.turn if value is None else value)

    def enter(self, j, stride):
        self.start, self.stride, self.turn = self.n, stride, j * stride

    def leave(self, turns):
        assert self.n == self.start + self.stride, (self.n - self.start, self.stride)
        self.n, self.turn = self.start + self.stride * turns, 0


def hybrid_mla_gdn_flow_block(nc, x, c, ctx, c_ctx, w_mod, b_mod, g_pre_mix, g_post_mix, g_pre_ffn, g_post_ffn, w_in,
            g_q_lora, w_uq, g_kv_lora, w_ukv, w_o_mla, conv_qkv, a_log, dt_bias, g_dn_out, w_o_dn,
            w_out, w_ffn_in, w_ffn_out, c_tri, c_levels, c_rope, out):
    stack = ExitStack()

    def sb(name, shape, dt=F32, where=None):
        return (where or stack).enter_context(nc.sbuf_tensor(name, shape, dt))

    def sem(name):
        return stack.enter_context(nc.semaphore(name))

    def dram(name, shape):
        return nc.dram_tensor(name, shape, F32, kind="Internal").ap()

    with stack:
        d_cq = dram("d_cq", (P, CQ // P, T))
        d_ckv = dram("d_ckv", (P, CKV // P, TA))
        d_v = dram("d_v", (P, DH, TA))
        d_z = dram("d_z", (P, DH, T))
        d_gate = dram("d_gate", (P, 2 * KD, T))
        d_x1 = dram("d_x1", (NT, P, D))

        ps = stack.enter_context(nc.psum_tensor("ps", [P, 8, HALF], F32))

        tri = sb("tri", [P, 6, P])
        ident, ones, tLE, tGE, tLT, tGT = (tri[:, n, :] for n in range(6))
        rope = sb("rope", [P, T])
        wraw = sb("wraw", [P, 2, KD, 2 * P])
        whi = sb("whi", [P, 2, KD, P], F32R)
        wlo = sb("wlo", [P, 2, KD, P], F32R)
        scb = sb("scb", [P, KD, 2])
        vrow = sb("vrow", [V_ROWS, P])
        vecs = sb("vecs", [P, V_ROWS])
        modv = sb("modv", [P, 4 * KD, 2])
        scale1 = sb("scale1", [P, KD, 2])
        scale2 = sb("scale2", [P, KD])
        gts = sb("gts", [P, 2 * KD])
        gpost = vrow[0:2 * KD]
        osum = sb("osum", [P, 4, NT])
        oroot = sb("oroot", [P, 3, NT])
        orcp = sb("orcp", [P, 3, NT])
        ss = sb("ss", [P, NA])
        lnt = sb("lnt", [P, NA])
        rstd = sb("rstd", [P, NA])
        eps = sb("eps", [P, 1])
        ba = sb("ba", [16, TA])
        krf = sb("krf", [ROPE, TA])
        bank = lambda b: ps[:, b, :]

        s_const = sem("s_const")
        s_x = [sem(f"s_x{n}") for n in range(NA // 2)]
        s_pair = [sem("s_pair0"), sem("s_pair1")]
        s_eps = sem("s_eps")
        s_vT = sem("s_vT")
        s_silu = sem("s_silu")
        s_mod = sem("s_mod")
        s_modv = sem("s_modv")
        s_ss = sem("s_ss")
        s_rstd = sem("s_rstd")
        s_xn = sem("s_xn")
        s_xT = sem("s_xT")
        s_u = sem("s_u")
        s_uhi = sem("s_uhi")
        s_ulo = sem("s_ulo")
        s_whi = sem("s_whi")
        s_wlo = sem("s_wlo")
        s_mm = sem("s_mm")
        s_ev = sem("s_ev")
        s_80 = sem("s_80")
        s_80hi = sem("s_80hi")
        s_80lo = sem("s_80lo")
        s_act = sem("s_act")
        s_dve = sem("s_dve")
        s_edge = sem("s_edge")
        s_ba = sem("s_ba")
        s_kr = sem("s_kr")
        s_sqc = sem("s_sqc")
        s_rawc = sem("s_rawc")
        s_sil = sem("s_sil")
        s_cqst = sem("s_cqst")
        s_ckvst = sem("s_ckvst")
        s_sq = sem("s_sq")
        s_sum = sem("s_sum")
        s_rs = sem("s_rs")
        s_nrm = sem("s_nrm")
        s_conv = sem("s_conv")
        s_st = [sem("s_st0"), sem("s_st1")]

        MODP = 8
        s_m2p = [sem("s_wp0"), sem("s_wp1")]
        s_slot = s_pair + s_m2p
        slot_of = lambda n: wraw[:, n // 2 % 2, :, (n % 2) * P:(n % 2 + 1) * P]
        MP0 = 16 * MODP // 2
        M2 = 16
        w_mod_v = w_mod.rearrange("a (k p) n -> p (a k) n", p=P)
        w_in_v = w_in.rearrange("a (k p) n -> p (a k) n", p=P)

        mid = ExitStack()
        qT = sb("qT", [P, DH, T], F32, mid)
        kT = sb("kT", [P, DH, TA], F32, mid)
        early = ExitStack()
        uhi = sb("uhi", [P, KD, TA], F32R, early)
        ulo = sb("ulo", [P, KD, TA], F32R, early)
        pre = ExitStack()
        xin = sb("xin", [P, NA, D], F32, pre)
        ut = kT[:, 0, 0:T].rearrange("p (a n) -> p a n", a=2)
        pre.close()
        p1 = ExitStack()
        craw = sb("craw", [P, 2, TA + 4], F32, p1)
        cy = sb("cy", [P, TA + 2], F32, p1)
        ys = sb("ys", [P, 2, TA], F32, p1)
        sqb = sb("sqb", [P, T], F32, p1)
        sqc = [ys[:, 0, h * TC:(h + 1) * TC] for h in range(2)] + [ys[:, 1, h * TC:(h + 1) * TC] for h in range(DH)]
        rs = sb("rs", [P, T], F32, p1)
        w80r = ys[:, 0, 2 * TC:2 * TC + KD * 48].rearrange("p (k n) -> p k n", k=KD)
        w80h = sb("w80h", [P, KD, 80], F32R, p1)
        w80l = sb("w80l", [P, KD, 80], F32R, p1)
        p1.close()
        early.close()
        dn = ExitStack()
        bankful = lambda name, n=1, dt=F32: sb(name, [P, 2, n, DH, P], dt, dn)
        levels = sb("levels", [P, 2, len(LEVELS), P], F32, dn)
        oT = sb("oT", [P, DH, T], F32, dn)
        dtb = sb("dtb", [P, 8], F32, dn)
        alog = sb("alog", [P, 8], F32, dn)
        beta = sb("beta", [P, NA, 8], F32, dn)
        gg = sb("gg", [P, NA, 8], F32, dn)
        gtmp = sb("gtmp", [P, 3, NA, 8], F32, dn)
        egs = sb("egs", [P, 3, 2, NA, DH], F32, dn)
        negeg = sb("negeg", [P, 2, NA, DH], F32, dn)
        lg = bankful("lg")
        dec = bankful("dec")
        decb = bankful("decb")
        eq = bankful("eq")
        qs = bankful("qs", 2)
        U = bankful("U")
        QK = bankful("QK", 2)
        e1 = bankful("e1")
        V = bankful("V", 2)
        VT = bankful("VT")
        Wt = bankful("Wt")
        vst = bankful("vst", 2)
        vt = bankful("vt")
        ks = bankful("ks")
        r1 = bankful("r1")
        rr = bankful("rr")
        vn = bankful("vn")
        S = bankful("S")
        Sg = bankful("Sg")
        dn.close()
        mid.close()

        STEPS = NA
        tile_at = [[NT + s if s < NC else s - NC for s in range(STEPS)],
                   [NA - 1 - s if s < NC else NT - 1 - (s - NC) for s in range(STEPS)]]
        NL = len(LEVELS) - 1
        PREP = 3 + 3 * NL - 1
        DECAY_AT = 15
        SCAN_AT = {1: 0, 4: 1, 8: 2, 12: 3}

        def schedule():
            for k in range(PREP):
                for d in range(2):
                    yield "prep", 0, d, k
            for d in range(2):
                yield "prep", 1, d, 0
            for s in range(STEPS):
                for k in range(PREP):
                    if k and s + 1 < STEPS:
                        for d in range(2):
                            yield "prep", s + 1, d, k
                    if k == DECAY_AT and s + 2 < STEPS:
                        for d in range(2):
                            yield "prep", s + 2, d, 0
                    if k in SCAN_AT:
                        for d in range(2):
                            yield "scan", s, d, SCAN_AT[k]
                    if k % 5 == 0 and 2 * s < M2:
                        yield "mod", 4 * s + k // 5, 0, 0

        def fills_of(what, s, d, k):
            a = 2 * d
            if what == "mod":
                return []
            if what == "scan":
                names = [["vT", "kT"], ["KS"] if s else [], ["X"], (["O"] if s >= NC else []) + ["SU"]][k]
                return [(name, None) for name in names]
            if k == 0:
                return [("DEC", a)] + ([("GC", a + 1)] if s >= NC else [])
            if k == 1:
                return [("KK", a)] + ([("KQ", a + 1)] if s >= NC else [])
            if k == 2:
                return [("TR", a)]
            return [[("W", a + 1)], [("H", a)], [("TR", a + 1)]][k % 3]

        fill = {}
        count = [0] * 8
        scan_fills = 0
        for what, s, d, k in schedule():
            for name, b in fills_of(what, s, d, k):
                if b is None:
                    b = 4 + scan_fills % 3
                    scan_fills += 1
                count[b] += 1
                fill[what, s, d, k, name] = (b, count[b])
        s_full = [sem(f"s_full{b}") for b in range(8)]

        def nth(d, n):
            return 2 * n - 1 + d

        s_lv = sem("s_lv")
        s_baT = sem("s_baT")
        s_beta = sem("s_beta")
        s_g = sem("s_g")
        s_lg, s_dec, s_eq, s_decm, s_decb, s_qs = map(sem, ("s_lg", "s_dec", "s_eq", "s_decm", "s_decb", "s_qs"))
        s_U, s_QK, s_e1, s_V, s_VT, s_Wt = map(sem, ("s_U", "s_QK", "s_e1", "s_V", "s_VT", "s_Wt"))
        s_vt, s_ks, s_r1, s_r, s_vn, s_S, s_Sg = map(sem, ("s_vt", "s_ks", "s_r1", "s_r", "s_vn", "s_S", "s_Sg"))
        s_vst = [sem("s_vst0"), sem("s_vst1")]
        s_oc = sem("s_oc")
        s_oa = sem("s_oa")

        def reader(what, s, d, k, name):
            lv = k // 3
            return {"DEC": (s_dec, nth(d, s + 1)), "GC": (s_eq, nth(d, s - NC + 1)), "KK": (s_U, nth(d, s + 1)),
                    "KQ": (s_QK, nth(d, s - NC + 1)), "TR": (s_VT, nth(d, NL * s + (1 if k == 2 else lv + 1))),
                    "W": (s_Wt, nth(d, NL * s + lv)), "H": (s_V, nth(d, (NL + 1) * s + 1 + lv)),
                    "vT": (s_vt, nth(d, s + 1)), "kT": (s_ks, nth(d, s + 1)), "KS": (s_r1, nth(d, s)),
                    "X": (s_vn, nth(d, s + 1)), "SU": (s_S, nth(d, s + 1)),
                    "O": (s_oc, 2 * (s - NC) + d + 1) if s < NC + 4 else (s_oa, 2 * (s - NC - 4) + d + 1)}[name]

        last_fill = {}
        seen = {}
        for key in fill:
            b = fill[key][0]
            last_fill[key] = seen.get(b)
            seen[b] = key

        att = ExitStack()
        qh = sb("qh", [QKD + 1, 2, T], F32R, att)
        ql = sb("ql", [QKD, 2, T], F32R, att)
        kh = sb("kh", [QKD + 1, 2, TA], F32R, att)
        kl = sb("kl", [QKD, 2, TA], F32R, att)
        vh = sb("vh", [P, 2, NA, 2 * VD], F32R, att)
        vl = sb("vl", [P, 2, NA, VD], F32R, att)
        ost = sb("ost", [VD, T], F32, att)
        rot = sb("rot", [P, 2, HALF], F32, att)
        rsum = sb("rsum", [P, HALF], F32, att)
        cqh, cql = (sb(n, [P, CQ // P, T], F32R, att) for n in ("cqh", "cql"))
        ckh, ckl = (sb(n, [P, CKV // P, TA], F32R, att) for n in ("ckh", "ckl"))
        Vf = sb("Vf", [P, NA, HEADS * VD], F32, att)
        pf = sb("pf", [P, T], F32, att)
        ph, pl = (sb(n, [P, 2, T], F32R, att) for n in ("ph", "pl"))
        mpad = sb("mpad", [P, NT, QKD + 1], F32, att)
        mx = sb("mx", [P, NT, 3], F32, att)
        krl = ost[0:ROPE, :]
        att.close()
        wflat = wraw[:].rearrange("p a k n -> p (a k n)")
        NQW = CQ // P * HEADS * QKD
        uq_raw = wflat[:, 0:NQW].rearrange("p (k n) -> p k n", k=CQ // P)
        uk_raw = wflat[:, NQW:NQW + CKV // P * HEADS * NOPE].rearrange("p (k h n) -> p k h n", k=CKV // P, h=HEADS)
        uv_raw = pf[:].rearrange("p (k n) -> p k n", k=CKV // P)
        uv_hi, uv_lo = (a[:, 0].rearrange("p (k n) -> p k n", k=CKV // P) for a in (ph, pl))
        vflat = Vf[:].rearrange("p t n -> p (t n)")
        ck_raw = vflat[:, 0:2 * TA].rearrange("p (k n) -> p k n", k=2)
        cq_raw = [vflat[:, 2 * TA:2 * TA + 2 * T].rearrange("p (k n) -> p k n", k=2),
                  vflat[:, 0:2 * T].rearrange("p (k n) -> p k n", k=2)]
        d_odn = dram("d_odn", (P, DH, T))
        d_oat = dram("d_oat", (HEADS, VD, T))
        d_g = dram("d_g", (2 * KD, P))

        s_gp, s_m2, s_grow, s_dg = map(sem, ("s_gp", "s_m2", "s_grow", "s_dg"))
        mg = ExitStack()
        oah, oal = (sb(n, [P, DH, T], F32R, mg) for n in ("oah", "oal"))
        sb("mg_gap0", [P, KD, T], F32, mg)
        odh, odl = (sb(n, [P, DH, T], F32R, mg) for n in ("odh", "odl"))
        gab = sb("gab", [P, 2, 2, T], F32, mg)
        sb("mg_gap1", [P, T], F32, mg)
        merged = sb("merged", [P, KD, T], F32, mg)
        mg.close()
        o_raw = gab[:].rearrange("p a b n -> p (a b) n")
        a_raw = merged[:, 0:DH]
        op = ExitStack()
        wo1 = [sb(n, [P, KD, HALF], F32R, op) for n in ("wo1h", "wo1l")]
        wo0 = [sb(n, [P, KD, HALF], F32R, op) for n in ("wo0h", "wo0l")]
        woh, wol = [wo0[0], wo1[0]], [wo0[1], wo1[1]]
        mth, mtl = (sb(n, [P, 2, KD, P], F32R, op) for n in ("mth", "mtl"))
        G1 = sb("G1", [P, D], F32, op)
        xt = sb("xt", [P, 2, D], F32, op)
        yt = sb("yt", [P, D], F32, op)
        xn = sb("xn", [P, D], F32, op)
        junk = sb("junk", [P, D], F32, op)
        op.close()
        ff = ExitStack()
        u2h, u2l = (sb(n, [P, KD, T], F32R, ff) for n in ("u2h", "u2l"))
        hid = sb("hid", [P, NFF, T], F32, ff)
        fjunk = sb("fjunk", [P, HALF], F32, ff)
        ff.close()
        f2 = ExitStack()
        hh, hl = (sb(n, [P, 2, T], F32R, f2) for n in ("hh", "hl"))
        f0 = sb("f0", [P, NT, HALF], F32, f2)
        x1 = sb("x1", [P, NT, D], F32, f2)
        f2.close()
        sg, G2 = rope, rope
        (s_md, s_mo, s_mh, s_ml, s_wh, s_wl, s_wm, s_mx, s_mg) = map(
            sem, ("s_md", "s_mo", "s_mh", "s_ml", "s_wh", "s_wl", "s_wm", "s_mx", "s_mg"))
        s_wp = s_m2p
        WP0 = 16 * (M2 + MODP) // 2
        s_gt = [sem("s_gt0"), sem("s_gt1")]
        s_rcx, s_fs = sem("s_rcx"), sem("s_fs")
        (s_G1, s_mth, s_mtl, s_o, s_ry, s_y, s_res, s_rx, s_xnt, s_tr, s_u2) = map(
            sem, ("s_G1", "s_mth", "s_mtl", "s_o", "s_ry", "s_y", "s_res", "s_rx", "s_xnt", "s_tr", "s_u2"))
        s_xt, XT0 = s_gt, 16 * KD // 2
        s_s1 = [sem("s_s10"), sem("s_s11")]
        (s_uh, s_ul, s_sg, s_h, s_gh, s_gl, s_fm, s_ft, s_f0, s_fq, s_rf, s_fy, s_out) = map(
            sem, ("s_uh", "s_ul", "s_sg", "s_h", "s_gh", "s_gl", "s_fm", "s_ft", "s_f0", "s_fq", "s_rf", "s_fy", "s_out"))
        s_fw, FW0 = s_wp, WP0 + 96 + 16 * NFF
        s_x1l = sem("s_x1l")
        W_O, W_FF = KD, 2 * KD
        W_ALL = W_FF + 2 * NFF
        d_gate_v = d_gate.rearrange("p (a k) n -> p a k n", a=2)

        def after_heads(eng):
            eng.wait_ge(s_ost, 16 * HEADS)

        def fill_last():
            b, n = fill_at(HEADS - 1, F_K + 2, 0)
            return s_pf[b], n
        (s_z, s_gsq, s_gsm, s_grs, s_gnrm, s_odn) = map(
            sem, ("s_z", "s_gsq", "s_gsm", "s_grs", "s_gnrm", "s_odn"))
        (s_uqk, s_uv, s_ck, s_cqa, s_hi, s_lo) = map(
            sem, ("s_uqk", "s_uv", "s_ck", "s_cqa", "s_hi", "s_lo"))
        (s_init, s_vp, s_vf, s_aw, s_av, s_qka, s_rd, s_rp, s_fin) = map(
            sem, ("s_init", "s_vp", "s_vf", "s_aw", "s_av", "s_qka", "s_rd", "s_rp", "s_fin"))
        s_pf = [sem("s_pf0"), sem("s_pf1")]
        s_pr = [sem("s_pr0"), sem("s_pr1")]
        (s_sf, s_ex, s_pl, s_pv, s_li, s_on, s_ost) = map(
            sem, ("s_sf", "s_ex", "s_pl", "s_pv", "s_li", "s_on", "s_ost"))
        AW = 12
        FILLS = 2 + 3 + 3 * NT + 2
        F_K, F_MAX, F_ROW = 2, 5, 5 + 3 * NT
        Q_AT, K_AT, M_FROM = [0, 1], [3, 4, 6], 9
        PLACES = [[] for _ in range(3 * NA)]
        for f, at in enumerate(Q_AT + K_AT):
            PLACES[at] = [f]
        for m in range(3 * NT):
            PLACES[M_FROM + m * (3 * NA - 2 - M_FROM) // (3 * NT)].append(F_MAX + m)
        PLACES[3 * NA - 1] = [F_ROW, F_ROW + 1]
        SLICES = [sum(PLACES[3 * kt:3 * kt + 3], []) for kt in range(NA)]

        def fill_at(head, f, j):
            g = FILLS * head + f
            return g % 2, g // 2 + 1 + FILLS * j

        def heads_loop(eng, one_head):
            for head in (0, 1):
                one_head(head, 0)
            with eng.Fori(0, (HEADS - 4) // 2) as j:
                for head in (2, 3):
                    one_head(head, j)
            for head in (HEADS - 2, HEADS - 1):
                one_head(head, 0)

        def after_deltanet(eng):
            eng.wait_ge(s_oa, 8)
            eng.wait_ge(s_S, nth(1, STEPS))

        def after_gating(eng):
            eng.wait_ge(s_odn, 16)

        def full(eng, key):
            b, n = fill[key]
            eng.wait_ge(s_full[b], n)
            return b

        def heads(b):
            return ps[:, b, :].rearrange("p (h n) -> p h n", h=DH)

        def per_head(a):
            return a.unsqueeze(2).broadcast_to([P, DH, P])

        def per_column(a):
            return a.unsqueeze(1).broadcast_to([P, DH, P])

        def after_projection(eng):
            eng.wait_ge(s_ev, len(steps))
            eng.wait_ge(s_mm, len(steps))
            for q in range(2):
                eng.wait_ge(s_st[q], 16 * 12)

        CH3 = [(0, HALF), (HALF, HALF), (T, TC)]
        CH2 = CH3[:2]
        steps = ([("cq", i) for i in range(4)] + [("ckv", i) for i in range(2)] + [("b", 0)]
                 + [("q", i) for i in range(4)] + [("k", i) for i in range(4)]
                 + [("v", i) for i in range(4)] + [("z", i) for i in range(4)]
                 + [("g", i) for i in range(16)])
        G0 = len(steps) - 16
        tile_steps = [n for n, (kind, _) in enumerate(steps) if kind != "b"]
        tile_of = {n: w for w, n in enumerate(tile_steps)}
        first = {"cq": 0, "ckv": O_CKV, "q": O_QKV, "k": O_QKV + 512, "v": O_QKV + 1024,
                 "z": O_Z, "g": O_GATE}
        NW1 = len(tile_steps)
        chunks_of = lambda kind: CH3 if kind in ("ckv", "b", "k", "v") else CH2
        sums = {}
        for n, (kind, i) in enumerate(steps):
            if kind in ("cq", "ckv", "q", "k"):
                last = {"cq": i == 3, "ckv": i == 1}.get(kind, True)
                sums[n + 1] = ("lat", kind, i, kind in "qk" or i == 0, last)
        at_ckvc = steps.index(("q", 0))
        at_kc = steps.index(("v", 1))
        sums[at_ckvc] = ("ckvc", "ckv", 0, True, True)
        sums[at_kc] = ("kc", "k", 0, True, True)
        n_sums = lambda n: sum(m <= n for m in sums)
        n_norms = lambda n: sum(m <= n and v[4] for m, v in sums.items())
        is_conv = lambda kind: kind in ("q", "k", "v")
        n_conv = lambda n: sum(is_conv(k) for k, _ in steps[:n])
        n_sq = lambda n: sum(k in ("cq", "ckv", "q", "k") for k, _ in steps[:n])
        n_out = lambda n: sum(k in ("v", "z", "g") for k, _ in steps[:n])
        two = lambda b: ps[:, b:b + 2, :].rearrange("p a n -> p (a n)")

        block = stack.enter_context(nc.Block())

        @block.sync
        def _(sp):
            sp.dma_start(tri[:], c_tri.rearrange("p (n q) -> p n q", q=P)).then_inc(s_const, 16)
            rows = ((0, c, "a (k p) -> (a k) p"), (8, c_ctx, "(k p) -> k p"), (16, b_mod, "a (k p) -> (a k) p"),
                    (V_G1, g_pre_mix, "a (k p) -> (a k) p"), (V_G2, g_pre_ffn, "a (k p) -> (a k) p"),
                    (V_GQ, g_q_lora, "a (k p) -> (a k) p"), (V_GKV, g_kv_lora, "a (k p) -> (a k) p"),
                    (V_CONV, conv_qkv, "a i (k p) -> (a i k) p"), (V_GDN, g_dn_out, "a p -> a p"))
            for at, src, how in rows:
                src = src.rearrange(how, p=P) if "(" in how else src
                sp.dma_start(vrow[at:at + src.shape[0], :], src).then_inc(s_const, 16)
            sp.dma_start(rope[:], c_rope).then_inc(s_const, 16)
            for a, g in enumerate((g_post_mix, g_post_ffn)):
                sp.wait_ge(s_vT, 1)
                sp.dma_start(gpost[a * KD:(a + 1) * KD], g.rearrange("a (k p) -> (a k) p", p=P)).then_inc(s_gp, 16)
            for n in range(2 * MODP):
                if n >= 4:
                    sp.wait_ge(s_mod, n - 3)
                sp.dma_start(slot_of(n), w_mod_v[:, :, n * P:(n + 1) * P]).then_inc(s_slot[n % 4], 16)

            def load_pair(n, src, j=0):
                if n < 2:
                    sp.wait_ge(s_mod, 2 * MODP - 2 + 2 * n)
                else:
                    sp.wait_ge(s_wlo, 2 * n - 2 + 4 * j)
                sp.dma_start(wraw[:, n % 2], src).then_inc(s_pair[n % 2], 16)

            NG = tile_of[G0] // 2
            for n in range(NG):
                kind, i = steps[tile_steps[2 * n]]
                col = first[kind] + i * P
                load_pair(n, w_in_v[:, :, col:col + 2 * P])
                if n == 0:
                    sp.wait_ge(s_xT, 24)
                    sp.dma_start(w80r[:, :, 0:ROPE], w_in_v[:, :, O_KR:O_KR + ROPE]).then_inc(s_80, 16)
                    sp.dma_start(w80r[:, :, ROPE:], w_in_v[:, :, O_BA:O_BA + 16]).then_inc(s_80, 16)
            with sp.Fori(0, 4) as j:
                for q in range(2):
                    load_pair(NG + q, w_in_v[:, :, bass.ds(j * 4 * P + (O_GATE + q * 2 * P), 2 * P)], j)

            after_projection(sp)
            sp.dma_start(levels[:], c_levels.rearrange("p (d l n) -> p d l n", d=2, l=len(LEVELS))).then_inc(s_lv, 16)
            sp.dma_start(dtb[:], dt_bias.rearrange("a d h -> a (d h)").broadcast_to([P, 8])).then_inc(s_lv, 16)
            sp.dma_start(alog[:], a_log.rearrange("a d h -> a (d h)").broadcast_to([P, 8])).then_inc(s_lv, 16)
            for s in range(STEPS):
                for n in (2 * s, 2 * s + 1) if 2 * s < M2 else ():
                    if n >= 2:
                        sp.wait_ge(s_m2, 2 * n - 2)
                    sp.dma_start(wraw[:, n % 2], w_mod_v[:, :, (MODP + n) * 256:(MODP + n + 1) * 256]).then_inc(s_m2p[n % 2], 16)
                for d in range(2):
                    if s >= 2:
                        full(sp, ("scan", s - 2, d, 0, "vT"))
                    t = tile_at[d][s]
                    sp.dma_start(vst[:, d, s % 2], d_v[:, :, t * P:(t + 1) * P]).then_inc(s_vst[s % 2], 16)

            after_deltanet(sp)
            sp.dma_start(ck_raw, d_ckv).then_inc(s_ck, 16)
            ukv = w_ukv.rearrange("a (k p) (h n) -> p (a k) h n", p=P, h=HEADS)
            for k in range(CKV // P):
                sp.dma_start(uv_raw[:, k].rearrange("p (h n) -> p h n", h=HEADS), ukv[:, k, :, NOPE:]).then_inc(s_uv, 16)
            sp.dma_start(kT[:, :, 0:T], d_z).then_inc(s_z, 16)
            sp.dma_start(cq_raw[0], d_cq[:, 0:2]).then_inc(s_cqa, 16)
            sp.wait_ge(s_lo, 1)
            sp.dma_start(cq_raw[1], d_cq[:, 2:4]).then_inc(s_ck, 16)
            sp.dma_start(uq_raw, w_uq.rearrange("a (k p) n -> p (a k) n", p=P)).then_inc(s_uqk, 16)
            for k in range(CKV // P):
                sp.dma_start(uk_raw[:, k], ukv[:, k, :, 0:NOPE]).then_inc(s_uqk, 16)
            sp.wait_ge(s_gnrm, 2 * DH)
            sp.dma_start(d_odn, oT[:]).then_inc(s_odn, 16)
            sp.wait_ge(s_grow, 2)
            sp.dma_start(d_g, gpost).then_inc(s_dg, 16)

            def store_x1(t):
                sp.wait_ge(s_res, t + 1)
                sp.dma_start(d_x1[t], xt[:, t % 2]).then_inc(s_s1[t % 2], 16)

            def store_head(head, j):
                if head == 0:
                    return
                sp.wait_ge(s_on, head + 2 * j)
                sp.dma_start(d_oat[bass.ds(2 * j + (head - 1), 1)].rearrange("a e n -> (a e) n"), ost[:]).then_inc(s_ost, 16)
            heads_loop(sp, store_head)

            sp.wait_ge(*fill_last())
            sp.dma_start(o_raw, d_odn).then_inc(s_md, 16)
            sp.wait_ge(s_aw, AW * HEADS)
            w_a, w_b = (w.rearrange("a (k p) n -> p (a k) n", p=P) for w in (w_o_mla, w_o_dn))

            def load_stream(n, parts):
                if n >= 2:
                    sp.wait_ge(s_wl, 2 * n - 2)
                for dst, src in parts:
                    sp.dma_start(dst, src).then_inc(s_wp[n % 2], 16)

            def load_merge(n):
                cols = slice(n * 2 * P, (n + 1) * 2 * P)
                load_stream(n, ((wraw[:, n % 2, 0:DH], w_a[:, :, cols]), (wraw[:, n % 2, DH:], w_b[:, :, cols])))
            load_merge(0)
            load_merge(1)
            store_head(HEADS, 0)
            after_heads(sp)
            sp.dma_start(a_raw, d_oat.rearrange("(t a) e n -> (a e) t n", a=2)).then_inc(s_mo, 16)
            for m in range(KD):
                if m >= 2:
                    sp.wait_ge(s_mg, m - 1)
                sp.dma_start(gab[:, m % 2], d_gate_v[:, :, m]).then_inc(s_gt[m % 2], 16)
                if m == 2:
                    load_merge(2)
                if m == 4:
                    load_merge(3)
            w_out_v = w_out.rearrange("a (k p) n -> p (a k) n", p=P)
            for n in range(4):
                load_stream(4 + n, ((wraw[:, n % 2], w_out_v[:, :, n * 2 * P:(n + 1) * 2 * P]),))
            sp.wait_ge(s_mg, KD)
            sp.wait_ge(s_dg, 16)
            sp.dma_start(G1[:], d_g[0:KD].rearrange("(a k) p -> a (k p)", a=1).broadcast_to([P, D])).then_inc(s_G1, 16)
            w_g, w_u = (w_ffn_in.rearrange("a (k p) n -> p (a k) n", p=P)[:, :, a * FF:(a + 1) * FF] for a in range(2))

            def load_ffn(i, j=0):
                q = i % 2
                at = bass.ds(2 * P * j + i * P, P)
                sp.wait_ge(s_wl, W_FF - 2 + 2 * i + 4 * j)
                for a, w in enumerate((w_g, w_u)):
                    sp.dma_start(wraw[:, q, :, a * P:(a + 1) * P], w[:, :, at]).then_inc(s_wp[q], 16)
            for t in range(NT):
                if t >= 2:
                    sp.wait_ge(s_s1[t % 2], 16 * (t // 2))
                    sp.wait_ge(s_xnt, t - 1)
                sp.dma_start(xt[:, t % 2], x[0, t * P:(t + 1) * P]).then_inc(s_xt[t % 2], 16)
                if t in (2, 3):
                    load_ffn(t - 2)
                if t:
                    store_x1(t - 1)
            store_x1(NT - 1)
            with sp.Fori(0, NFF // 2 - 1) as j:
                for i in (2, 3):
                    load_ffn(i, j)
            def load_f2(half, k, j=0):
                m = NFF * half + k
                if m < 2:
                    sp.wait_ge(s_wl, W_ALL)
                else:
                    sp.wait_ge(s_gl, m - 1 + 2 * j)
                at = bass.ds(2 * P * j + k * P, P)
                sp.dma_start(wraw[:, m % 2, 0:2].rearrange("p a n -> p (a n)"),
                             w_ffn_out[0, at, half * HALF:(half + 1) * HALF]).then_inc(s_fw[m % 2], 16)
            for half in range(2):
                load_f2(half, 0)
                load_f2(half, 1)
                if half == 0:
                    sp.wait_ge(s_h, NFF)
                    sp.wait_ge(s_wm, KD + 2 * NFF)
                    for q in range(2):
                        sp.wait_ge(s_s1[q], 16 * NT // 2)
                    sp.dma_start(G2[:], d_g[KD:].rearrange("(a k) p -> a (k p)", a=1).broadcast_to([P, D])).then_inc(s_G1, 16)
                    sp.dma_start(x1[:], d_x1.rearrange("t p n -> p t n")).then_inc(s_x1l, 16)
                with sp.Fori(0, NFF // 2 - 1) as j:
                    for k in (2, 3):
                        load_f2(half, k, j)
            for t in range(NT):
                sp.wait_ge(s_fy, 3 * (t + 1))
                sp.dma_start(out[0, t * P:(t + 1) * P], x1[:, t]).then_inc(s_out, 16)
            sp.wait_ge(s_out, 16 * NT)

        @block.gpsimd
        def _(pool):
            pool.memset(eps[:], EPS).then_inc(s_eps, 1)
            for n in range(2):
                pool.dma_start(xin[:, n], x[0, n * P:(n + 1) * P]).then_inc(s_x[n // 2], 16)
            for n in range(2, NA):
                src = x[0, n * P:(n + 1) * P] if n < NT else ctx[0, (n - NT) * P:(n - NT + 1) * P]
                pool.dma_start(xin[:, n], src).then_inc(s_x[n // 2], 16)
            pool.wait_ge(s_xT, 24)
            for q in range(2):
                for col in (0, T + 1, T + 2, TA + 3):
                    pool.memset(craw[:, q, col:col + 1], 0.0).then_inc(s_edge, 1)
            pool.wait_ge(s_nrm, 1)
            pool.dma_start(d_cq, qT[:]).then_inc(s_cqst, 16)
            pool.wait_ge(s_nrm, 3)
            pool.dma_start(d_ckv, kT[:, 0:2, :]).then_inc(s_ckvst, 16)

            after_projection(pool)
            pool.wait_ge(s_lv, 48)
            pool.wait_ge(s_beta, 3)

            def log_decays(s, d):
                if s:
                    full(pool, ("prep", s - 1, d, 1, "KK"))
                pool.tensor_tensor(lg[:, d, 0], per_column(tLE if d == 0 else tGE),
                                   per_head(gg[:, tile_at[d][s], 4 * d:4 * d + 4]), ALU.mult).then_inc(s_lg, 1)

            for what, s, d, k in schedule():
                if what == "mod":
                    continue
                t = tile_at[d][s]
                if what == "prep" and k == 2 and s + 1 < STEPS:
                    log_decays(s + 1, d)
                if what == "prep" and k == 0:
                    if s == 0:
                        log_decays(0, d)
                    pool.wait_ge(s_dec, nth(d, s + 1))
                    pool.tensor_tensor(dec[:, d, 0], dec[:, d, 0], per_column(tLE if d == 0 else tGE),
                                       ALU.mult).then_inc(s_decm, 1)
                    pool.wait_ge(s_decm, nth(d, s + 1))
                    pool.tensor_tensor(decb[:, d, 0], dec[:, d, 0], per_head(beta[:, t, 4 * d:4 * d + 4]),
                                       ALU.mult).then_inc(s_decb, 1)
                    if s >= NC:
                        pool.wait_ge(s_eq, nth(d, s - NC + 1))
                        if s >= NC + 2:
                            full(pool, ("scan", s - 2, d, 3, "O"))
                        pool.tensor_tensor(qs[:, d, s % 2], qT[:, :, t * P:(t + 1) * P], eq[:, d, 0], ALU.mult).then_inc(s_qs, 1)
                elif what == "prep" and k == 1:
                    pool.wait_ge(s_U, nth(d, s + 1))
                    pool.tensor_tensor(e1[:, d, 0], U[:, d, 0], per_column(levels[:, 1 - d, 0]), ALU.mult).then_inc(s_e1, 1)
                elif what == "scan" and k == 1 and s:
                    pool.wait_ge(s_S, nth(d, s))
                    pool.tensor_tensor(Sg[:, d, 0], S[:, d, 0], per_head(egs[:, 2, d, t]), ALU.mult).then_inc(s_Sg, 1)

            def split_weights(head):
                p = head % 2
                if head == 1:
                    pool.wait_ge(s_av, 2)
                elif head:
                    pool.wait_ge(s_rp, 6 * head)
                if head >= 2:
                    b, n = fill_at(head - 2, F_K + 2, 0)
                    pool.wait_ge(s_pf[b], n)
                qc = uq_raw[:, :, QKD * head:QKD * (head + 1)]
                kc = uk_raw[:, :, head]
                qwh, qwl = whi[:, p, 0:4], wlo[:, p, 0:4]
                kwh, kwl = (w[:, p, 4].rearrange("p (k n) -> p k n", k=CKV // P) for w in (whi, wlo))
                for n, (raw, hi) in enumerate(((qc, qwh[:, :, 0:QKD]), (kc, kwh))):
                    pool.tensor_copy(hi, raw).then_inc(s_aw, 1)
                for a in range(2):
                    for h in range(2):
                        src = NOPE + 16 * a + 8 * (1 - h)
                        dst = QKD + 16 * a + 8 * h
                        raw = uq_raw[:, :, QKD * head + src:QKD * head + src + 8]
                        pool.tensor_copy(qwh[:, :, dst:dst + 8], raw).then_inc(s_aw, 1)
                pool.wait_ge(s_aw, AW * head + 6)
                for raw, hi, lo in ((qc, qwh[:, :, 0:QKD], qwl[:, :, 0:QKD]), (kc, kwh, kwl)):
                    pool.tensor_tensor(lo, raw, hi.bitcast(F32), ALU.subtract).then_inc(s_aw, 1)
                for a in range(2):
                    for h in range(2):
                        src = NOPE + 16 * a + 8 * (1 - h)
                        dst = slice(QKD + 16 * a + 8 * h, QKD + 16 * a + 8 * h + 8)
                        raw = uq_raw[:, :, QKD * head + src:QKD * head + src + 8]
                        pool.tensor_tensor(qwl[:, :, dst], raw, qwh[:, :, dst].bitcast(F32), ALU.subtract).then_inc(s_aw, 1)

            def split_values(head):
                p = head % 2
                if head == 0:
                    pool.wait_ge(s_vf, NA)
                    pool.wait_ge(s_rp, 6)
                if head >= 2:
                    pool.wait_ge(s_pv, NA * (head - 1))
                vsrc = Vf[:, :, VD * head:VD * (head + 1)]
                pool.tensor_copy(vh[:, p, :, 0:VD], vsrc).then_inc(s_av, 1)
                pool.wait_ge(s_av, 2 * head + 1)
                pool.tensor_tensor(vl[:, p], vsrc, vh[:, p, :, 0:VD].bitcast(F32), ALU.subtract).then_inc(s_av, 1)

            def rotary_sums(head):
                p = head % 2
                for c in range(2):
                    tok = slice(c * HALF, (c + 1) * HALF)
                    n = 2 * head + c
                    pool.wait_ge(s_rd, n + 1)
                    if c:
                        pool.wait_ge(s_rp, 3 * n)
                    elif head:
                        pool.wait_ge(s_av, 2 * (head + 1))
                    else:
                        pool.wait_ge(s_init, 3)
                    pool.tensor_tensor(rsum[NOPE:QKD], rot[NOPE:QKD, 0], rot[NOPE:QKD, 1], ALU.add).then_inc(s_rp, 1)
                    pool.wait_ge(s_rp, 3 * n + 1)
                    pool.tensor_copy(qh[NOPE:QKD, p, tok], rsum[NOPE:QKD]).then_inc(s_rp, 1)
                    pool.wait_ge(s_rp, 3 * n + 2)
                    pool.tensor_tensor(ql[NOPE:QKD, p, tok], rsum[NOPE:QKD], qh[NOPE:QKD, p, tok].bitcast(F32),
                                       ALU.subtract).then_inc(s_rp, 1)

            pool.wait_ge(s_uqk, 48)
            split_weights(0)
            pool.wait_ge(s_aw, AW)
            after_gating(pool)
            pool.memset(mpad[:], 0.0).then_inc(s_init, 1)
            pool.wait_ge(s_init, 1)
            pool.memset(kh[QKD:QKD + 1].bitcast(F32), 1.0).then_inc(s_init, 1)
            pool.wait_ge(s_init, 2)
            pool.memset(vh[:, :, :, VD:].bitcast(F32), 1.0).then_inc(s_init, 1)
            rotary_sums(0)
            split_values(0)
            for head in range(1, HEADS):
                split_weights(head)
                split_values(head)
                rotary_sums(head)

        @block.scalar
        def _(act):
            act.wait_ge(s_vT, 1)
            act.activation(vecs[:], ps[:, 7, 0:V_ROWS], ACT.Copy).then_inc(s_silu, 1)
            act.wait_ge(s_silu, 1)
            act.activation(scb[:], vecs[:, 0:2 * KD].rearrange("p (a k) -> p k a", a=2), ACT.Silu).then_inc(s_silu, 1)
            for n in range(NA):
                act.wait_ge(s_x[n // 2], 32)
                if n >= KD:
                    act.wait_ge(s_ss, n - KD + 1)
                act.activation(uhi[:, n % KD, 0:D], xin[:, n], ACT.Square, accum_out=ss[:, n:n + 1]).then_inc(s_ss, 1)
            act.wait_ge(s_eps, 1)
            act.wait_ge(s_ss, NA)
            act.activation(lnt[:], ss[:], ACT.Ln, bias=eps[:, 0:1], scale=1.0 / D).then_inc(s_ss, 1)
            act.wait_ge(s_ss, NA + 1)
            act.activation(rstd[:], lnt[:], ACT.Exp, scale=-0.5).then_inc(s_rstd, 1)
            act.wait_ge(s_modv, 2)
            for n in range(24):
                g, k = divmod(n, KD)
                w = HALF if g < 2 else TC
                act.wait_ge(s_xT, n + 1)
                if n >= 2:
                    act.wait_ge(s_ulo, n - 1)
                act.activation(ut[:, n % 2, 0:w], ps[:, 1 + n % 4, 0:w], ACT.Identity,
                               bias=modv[:, k, g // 2:g // 2 + 1], scale=scale1[:, k, g // 2:g // 2 + 1]).then_inc(s_u, 1)

            own = Own(act, s_act)

            def split_hi(n, j=0):
                w = tile_of.get(n)
                if w is None:
                    act.wait_ge(s_80, 32)
                    kr = w80r[:, :, 0:ROPE].rearrange("p k (a s f) -> p k a s f", a=2, s=2)
                    rot = w80h[:, :, ROPE:2 * ROPE].rearrange("p k (a s f) -> p k a s f", a=2, s=2)
                    act.activation(w80h[:, :, 0:ROPE], w80r[:, :, 0:ROPE], ACT.Copy).then_inc(s_80hi, 1)
                    act.activation(w80h[:, :, 64:80], w80r[:, :, ROPE:], ACT.Copy).then_inc(s_80hi, 1)
                    for a in range(2):
                        for h in range(2):
                            act.activation(rot[:, :, a, h], kr[:, :, a, 1 - h], ACT.Copy).then_inc(s_80hi, 1)
                    return
                slot = (w // 2) % 2
                act.wait_ge(s_pair[slot], 16 * ((w // 2) // 2 + 1 + MODP // 2) + 16 * j)
                if w >= 2:
                    act.wait_ge(s_mm, tile_steps[w - 2] + 1 + 4 * j)
                act.activation(whi[:, w % 2], wraw[:, slot, :, (w % 2) * P:(w % 2 + 1) * P], ACT.Copy).then_inc(s_whi, 1)

            def norm(n):
                if n not in sums or not sums[n][4]:
                    return
                what, kind = sums[n][:2]
                width, inv = TC if what == "ckvc" else T, {"cq": 1 / CQ, "ckv": 1 / CKV}.get(kind, 1.0)
                act.wait_ge(s_sum, n_sums(n))
                if n_norms(n) > 1:
                    act.wait_ge(s_nrm, n_norms(n) - 1)
                act.activation(rs[:, 0:width], two(6)[:, 0:width], ACT.Ln, bias=eps[:, 0:1], scale=inv).then_inc(s_rs, 1)
                act.wait_ge(s_rs, 2 * n_norms(n) - 1)
                act.activation(rs[:, 0:width], rs[:, 0:width], ACT.Exp, scale=-0.5).then_inc(s_rs, 1)

            def squares(n, src, kind, i):
                own.wait()
                if n_sums(n):
                    act.wait_ge(s_sum, n_sums(n))
                if kind in ("ckv", "k"):
                    act.activation(sqc[i + (2 if kind == "k" else 0)], src[:, i, T:], ACT.Square).then_inc(s_sqc, 1)
                act.activation(sqb[:, :], src[:, i, 0:T], ACT.Square).then_inc(s_sq, 1)

            def evac(n, j=0):
                kind, i = steps[n]
                base = 3 * (n % 2)
                act.wait_ge(s_mm, n + 1 + 4 * j)
                if kind in ("cq", "ckv"):
                    dst = qT if kind == "cq" else kT
                    if kind == "ckv":
                        own.mark(act.activation(dst[:, i, T:], ps[:, base + 2, 0:TC], ACT.Copy))
                    act.activation(dst[:, i, 0:T], two(base), ACT.Copy).then_inc(s_ev, 1)
                    act.wait_ge(s_ev, n + 1)
                    squares(n, dst, kind, i)
                elif kind == "b":
                    act.activation(ba[:, T:], ps[64:80, base + 2, 0:TC], ACT.Copy).then_inc(s_ba, 1)
                    act.activation(krf[:, T:], ps[0:ROPE, base + 2, 0:TC], ACT.Copy).then_inc(s_ba, 1)
                    act.activation(ba[:, 0:T], two(base)[64:80], ACT.Copy).then_inc(s_ev, 1)
                elif is_conv(kind):
                    m = n_conv(n)
                    if m == 0:
                        act.wait_ge(s_edge, 8)
                    if m >= 2:
                        act.wait_ge(s_conv, m - 1)
                    if kind != "q":
                        act.activation(craw[:, m % 2, T + 3:TA + 3], ps[:, base + 2, 0:TC], ACT.Copy).then_inc(s_rawc, 1)
                    act.activation(craw[:, m % 2, 1:T + 1], two(base), ACT.Copy).then_inc(s_ev, 1)
                    if kind in "qk" and i == 0:
                        act.wait_ge(s_cqst if kind == "q" else s_ckvst, 16)
                    act.wait_ge(s_conv, m + 1)
                    if kind == "v":
                        o = n_out(n)
                        if o >= 2:
                            act.wait_ge(s_st[o % 2], 16 * (o // 2))
                        if o == 1:
                            act.wait_ge(s_sum, n_sums(at_kc))
                        own.mark(act.activation(ys[:, o % 2, 0:T], cy[:, 0:T], ACT.Silu))
                        act.activation(ys[:, o % 2, T:], cy[:, T + 2:TA + 2], ACT.Silu).then_inc(s_sil, 1)
                        own.wait()
                        act.wait_ge(s_sil, m + 1)
                        act.dma_start(d_v[:, i, :], ys[:, o % 2, :]).then_inc(s_st[o % 2], 16)
                    else:
                        dst = qT if kind == "q" else kT
                        if kind == "k":
                            own.mark(act.activation(dst[:, i, T:], cy[:, T + 2:TA + 2], ACT.Silu))
                        act.activation(dst[:, i, 0:T], cy[:, 0:T], ACT.Silu).then_inc(s_sil, 1)
                        act.wait_ge(s_sil, m + 1)
                        squares(n, dst, kind, i)
                else:
                    o = n_out(n)
                    act.wait_ge(s_st[o % 2], 16 * (o // 2) + 32 * j)
                    act.activation(ys[:, o % 2, 0:T], two(base), ACT.Silu if kind == "z" else ACT.Sigmoid).then_inc(s_ev, 1)
                    act.wait_ge(s_ev, n + 1 + 4 * j)
                    dst = d_z[:, i, :] if kind == "z" else d_gate[:, bass.ds(4 * j + i, 1), :].rearrange("p a n -> p (a n)")
                    act.dma_start(dst, ys[:, o % 2, 0:T]).then_inc(s_st[o % 2], 16)

            split_hi(0)
            for n in range(G0 + 2):
                split_hi(n + 1)
                norm(n - 1)
                if n:
                    evac(n - 1)
            with act.Fori(0, 3) as j:
                for n in range(G0 + 2, G0 + 6):
                    split_hi(n + 1, j)
                    evac(n - 1, j)
            split_hi(G0 + 15)
            evac(G0 + 13)
            evac(G0 + 14)
            evac(G0 + 15)
            for q in range(2):
                act.wait_ge(s_st[q], 16 * 12)

            after_projection(act)
            act.wait_ge(s_baT, 1)
            ba_t = ps[:, 0, 0:NA * 16].rearrange("p (t n) -> p t n", t=NA)
            act.activation(beta[:], ba_t[:, :, 0:8], ACT.Sigmoid).then_inc(s_beta, 1)
            act.wait_ge(s_lv, 48)
            own.mark(act.activation(alog[:], alog[:], ACT.Exp))
            own.wait()
            act.wait_ge(s_g, 1)
            own.mark(act.activation(gtmp[:, 2], gtmp[:, 2], ACT.Exp))
            own.wait()
            act.activation(gtmp[:, 2], gtmp[:, 2], ACT.Ln, bias=ones[:, 0:1]).then_inc(s_beta, 1)
            act.wait_ge(s_baT, 2)
            act.activation(egs[:], ps[:, 1, 0:6 * NA * DH].rearrange("p (a d t h) -> p a d t h", a=3, d=2, t=NA),
                           ACT.Exp).then_inc(s_beta, 1)
            for what, s, d, k in schedule():
                key = (what, s, d, k)
                if what == "prep" and k == 0:
                    b = full(act, (*key, "DEC"))
                    if s:
                        act.wait_ge(s_U, nth(d, s))
                        if s > NC:
                            act.wait_ge(s_QK, nth(d, s - NC))
                        act.wait_ge(s_decb, nth(d, s))
                    act.activation(dec[:, d, 0], heads(b), ACT.Exp).then_inc(s_dec, 1)
                    if s >= NC:
                        b = full(act, (*key, "GC"))
                        if s > NC:
                            act.wait_ge(s_qs, nth(d, s - NC))
                        act.activation(eq[:, d, 0], heads(b), ACT.Exp).then_inc(s_eq, 1)
                elif what == "prep" and (k == 2 or k % 3 == 2):
                    b = full(act, (*key, "TR"))
                    act.activation(VT[:, d, 0], heads(b), ACT.Copy).then_inc(s_VT, 1)
                elif what == "scan" and k == 0:
                    b = full(act, (*key, "vT"))
                    if s:
                        act.wait_ge(s_r, nth(d, s))
                    act.activation(vt[:, d, 0], heads(b), ACT.Copy).then_inc(s_vt, 1)
                elif what == "scan" and k == 3 and NC <= s < NC + 4:
                    t = tile_at[d][s]
                    b = full(act, (*key, "O"))
                    act.activation(oT[:, :, t * P:(t + 1) * P], heads(b), ACT.Copy).then_inc(s_oc, 1)

            after_deltanet(act)
            for h in range(DH):
                act.activation(qT[:, h], oT[:, h], ACT.Square).then_inc(s_gsq, 1)

            act.wait_ge(s_ck, 16)
            act.activation(ckh[:], ck_raw, ACT.Copy).then_inc(s_hi, 1)
            act.wait_ge(s_uv, 32)
            act.activation(uv_hi, uv_raw, ACT.Copy).then_inc(s_hi, 1)
            act.preload_act_table_set("natural_log_exp_and_others")
            for h in range(DH):
                act.wait_ge(s_gsm, h + 1)
                act.activation(qT[:, h], two(2 * h), ACT.Ln, bias=eps[:, 0:1], scale=1.0 / DK).then_inc(s_grs, 1)
            for h in range(DH):
                act.wait_ge(s_grs, h + 1)
                act.activation(qT[:, h], qT[:, h], ACT.Exp, scale=-0.5).then_inc(s_grs, 1)
            for n, landed in enumerate(((s_cqa, 16), (s_ck, 32))):
                act.wait_ge(*landed)
                act.activation(cqh[:, 2 * n:2 * n + 2], cq_raw[n], ACT.Copy).then_inc(s_hi, 1)
            act.wait_ge(s_lo, 4)
            for t in range(NA):
                act.wait_ge(s_vp, t + 1)
                act.activation(Vf[:, t], ps[:, t % 4, :], ACT.Copy).then_inc(s_vf, 1)
            after_gating(act)

            def prepare(head, j, fills):
                p = head % 2
                for f in fills:
                    b, n = fill_at(head, f, j)
                    if f < F_K:
                        act.wait_ge(s_pf[b], n)
                        act.activation(qh[0:NOPE, p, f * HALF:(f + 1) * HALF], ps[0:NOPE, 6 + b, :], ACT.Copy).then_inc(s_qka, 1)
                    elif f < F_MAX:
                        t0, tw = CH3[f - F_K]
                        act.wait_ge(s_pf[b], n)
                        act.activation(kh[0:NOPE, p, t0:t0 + tw], ps[0:NOPE, 6 + b, 0:tw], ACT.Copy).then_inc(s_qka, 1)
                    elif f >= F_ROW:
                        c = f - F_ROW
                        act.wait_ge(s_pf[b], n)
                        act.activation(qh[QKD:QKD + 1, p, c * HALF:(c + 1) * HALF], ps[QKD:QKD + 1, 6 + b, :],
                                       ACT.Copy, scale=-1.0).then_inc(s_pr[b], 1)

            def finish(head, j):
                act.wait_ge(s_pv, NA * (head + 1 + 2 * j))
                if head:
                    act.wait_ge(s_ost, 16 * (head + 2 * j))
                act.activation(ost[:], two(4)[VD:P], ACT.Ln).then_inc(s_li, 1)
                act.wait_ge(s_li, 2 * head + 1 + 4 * j)
                act.activation(ost[:], ost[:], ACT.Exp, scale=-1.0).then_inc(s_li, 1)

            def one_head(head, j):
                for kt in range(NA):
                    n = NA * (head + 2 * j) + kt
                    act.wait_ge(s_sf, n + 1)
                    if head or kt >= 2:
                        act.wait_ge(s_pv, n - 1)
                    b = 2 * (kt % 2)
                    act.activation(ph[:, kt % 2], two(b), ACT.Exp, scale=QKD ** -0.5)
                    if head or kt:
                        act.wait_ge(s_pl, n)
                    act.activation(pf[:], two(b), ACT.Exp, scale=QKD ** -0.5).then_inc(s_ex, 1)
                    if kt == 0 and head:
                        finish(head - 1, j)
                    if head < HEADS - 1:
                        prepare(head + 1, j, SLICES[kt])
                    elif kt == 4:
                        act.wait_ge(s_md, 16)
                        act.activation(odh[:], o_raw, ACT.Copy).then_inc(s_mh, 1)
                    elif kt in (6, 8):
                        stream_hi(kt // 2 - 3)

            def stream_hi(w, j=0, dst=None):
                if w < W_O:
                    act.wait_ge(s_wp[w // 2 % 2], WP0 + 32 * (w // 4 + 1))
                elif w < W_FF:
                    act.wait_ge(s_wp[w // 2 % 2], WP0 + 64 + 16 * ((w - W_O) // 4 + 1))
                else:
                    act.wait_ge(s_wp[w // 2 % 2], WP0 + 96 + 32 * ((w - W_FF) // 4 + 1) + 32 * j)
                if w < 2:
                    act.wait_ge(*fill_last())
                elif w < W_O:
                    act.wait_ge(s_wm, w - 1)
                elif W_O + 4 <= w < W_FF:
                    act.wait_ge(s_wm, W_O)
                elif w >= W_FF + 2:
                    act.wait_ge(s_wm, w - W_O - 1 + 4 * j)
                act.activation(whi[:, w % 2] if dst is None else dst,
                               wraw[:, w // 2 % 2, :, (w % 2) * P:(w % 2 + 1) * P], ACT.Copy).then_inc(s_wh, 1)

            prepare(0, 0, range(F_MAX))
            for p in range(2):
                act.activation(kh[NOPE:QKD, p], krf[:], ACT.Copy).then_inc(s_hi, 1)
            prepare(0, 0, range(F_MAX, FILLS))
            heads_loop(act, one_head)
            finish(HEADS - 1, 0)

            act.wait_ge(s_ml, 1)
            act.wait_ge(s_mo, 16)
            act.activation(oah[:], a_raw, ACT.Copy).then_inc(s_mh, 1)
            for w in range(2, W_O):
                stream_hi(w)
            def out_hi(c):
                for w in range(W_O + 4 * c, W_O + 4 * c + 4):
                    stream_hi(w, dst=woh[c][:, :, (w % 4) * P:(w % 4 + 1) * P])

            def token_hi(t):
                if t == 0:
                    act.wait_ge(s_mg, KD)
                if t >= 2:
                    act.wait_ge(s_o, t - 1)
                act.activation(mth[:, t % 2], merged[:, :, t * P:(t + 1) * P], ACT.Copy).then_inc(s_mth, 1)

            def mean_root(src, n, t, s_of):
                if n:
                    act.wait_ge(s_ry, 2 * t + 1)
                elif t:
                    act.wait_ge(s_rx, 2 * t - 1)
                act.activation(junk[:], src, ACT.Square, accum_out=osum[:, n, t:t + 1]).then_inc(s_of, 1)
                act.wait_ge(s_of, 2 * t + 1)
                act.activation(oroot[:, n, t:t + 1], osum[:, n, t:t + 1], ACT.Sqrt, bias=eps[:, 0:1], scale=1.0 / D).then_inc(s_of, 1)

            out_hi(0)
            token_hi(0)
            out_hi(1)
            token_hi(1)
            for t in range(NT):
                act.wait_ge(s_o, t + 1)
                mean_root(two(2 * (t % 3)), 0, t, s_ry)
                if t + 2 < NT:
                    token_hi(t + 2)
                act.wait_ge(s_res, t + 1)
                mean_root(xt[:, t % 2], 1, t, s_rx)
                act.wait_ge(s_rcx, t + 1)
                if t:
                    act.wait_ge(s_tr, t)
                act.activation(xn[:], xt[:, t % 2], ACT.Copy, scale=orcp[:, 1, t:t + 1]).then_inc(s_xnt, 1)
            act.wait_ge(s_o, NT)
            stream_hi(W_FF)
            act.wait_ge(s_u2, NT)
            for c in range(2):
                for k0 in range(0, KD, 2):
                    at = (slice(None), slice(k0, k0 + 2), slice(c * HALF, (c + 1) * HALF))
                    act.activation(u2h[at], merged[at], ACT.Copy).then_inc(s_uh, 1)
                if c == 0:
                    stream_hi(W_FF + 1)

            def gate(i, j=0):
                if i + 1 < NFF:
                    stream_hi(W_FF + 2 * i + 2, j)
                act.wait_ge(s_wm, KD + 2 * i + 1 + 2 * 2 * j)
                if i:
                    act.wait_ge(s_h, i + 2 * j)
                act.activation(sg[:], two(4 * (i % 2)), ACT.Silu).then_inc(s_sg, 1)
                if i + 1 < NFF:
                    stream_hi(W_FF + 2 * i + 3, j)
            gate(0)
            with act.Fori(0, NFF // 2 - 1) as j:
                gate(1, j)
                gate(2, j)
            gate(NFF - 1)

            def split_f2(half, k, j=0):
                m = NFF * half + k
                act.wait_ge(s_fw[m % 2], FW0 + 16 * (m // 2 + 1) + 16 * j)
                if m == 0:
                    act.wait_ge(s_wm, KD + 2 * NFF)
                    act.wait_ge(s_h, NFF)
                if half and k < 2:
                    act.wait_ge(s_ft, NT)
                elif m >= 2:
                    act.wait_ge(s_fm, m - 1 - 2 * half + 2 * j)
                act.activation(whi[:, m % 2, 0:4].rearrange("p a n -> p (a n)"),
                               wraw[:, m % 2, 0:2].rearrange("p a n -> p (a n)"), ACT.Copy)
                act.activation(hh[:, m % 2], hid[:, bass.ds(2 * j + k, 1)].rearrange("p a n -> p (a n)"), ACT.Copy).then_inc(s_gh, 1)

            def half_squares(half, t):
                act.wait_ge(s_ft, NT * half + t + 1)
                if t or half:
                    act.wait_ge(s_fq, NT * half + t)
                act.activation(fjunk[:], ps[:, t, :], ACT.Square, accum_out=osum[:, 2 + half, t:t + 1]).then_inc(s_fq, 1)

            for half in range(2):
                if half:
                    for t in range(NT):
                        half_squares(0, t)
                split_f2(half, 0)
                split_f2(half, 1)
                with act.Fori(0, NFF // 2 - 1) as j:
                    for k in (2, 3):
                        split_f2(half, k, j)
            for t in range(NT):
                half_squares(1, t)
                act.wait_ge(s_fs, t + 1)
                act.activation(oroot[:, 2, t:t + 1], osum[:, 3, t:t + 1], ACT.Sqrt, bias=eps[:, 0:1], scale=1.0 / D).then_inc(s_rf, 1)

        @block.vector
        def _(dve):
            own = Own(dve, s_dve)
            dve.wait_ge(s_mod, 2 * MODP)
            dve.tensor_tensor(modv[:, 0:2 * KD], ps[:, 0, 0:4 * KD].rearrange("p (k a) -> p k a", a=2),
                              vecs[:, V_BMOD:V_BMOD + 2 * KD].unsqueeze(2).broadcast_to([P, 2 * KD, 2]), ALU.add).then_inc(s_modv, 1)
            dve.wait_ge(s_modv, 1)
            own.mark(dve.tensor_scalar(scale1[:], modv[:, KD:2 * KD], 1.0, None, ALU.add))
            own.wait()
            dve.tensor_tensor(scale1[:], scale1[:], vecs[:, V_G1:V_G1 + KD].unsqueeze(2).broadcast_to([P, KD, 2]),
                              ALU.mult).then_inc(s_modv, 1)
            dve.wait_ge(s_rstd, 1)
            for n in range(NA):
                dve.tensor_scalar(xin[:, n], xin[:, n], rstd[:, n:n + 1], None, ALU.mult).then_inc(s_xn, 1)
            for n in range(24):
                g, k = divmod(n, KD)
                w = HALF if g < 2 else TC
                dst = (slice(None), k, slice(g * HALF, g * HALF + w))
                dve.wait_ge(s_u, n + 1)
                own.mark(dve.tensor_copy(uhi[dst], ut[:, n % 2, 0:w]))
                own.wait()
                dve.tensor_tensor(ulo[dst], ut[:, n % 2, 0:w], uhi[dst].bitcast(F32), ALU.subtract).then_inc(s_ulo, 1)

            def split_lo(n, j=0):
                w = tile_of.get(n)
                if w is None:
                    dve.wait_ge(s_80hi, 6)
                    kr = w80r[:, :, 0:ROPE].rearrange("p k (a s f) -> p k a s f", a=2, s=2)
                    parts = [(slice(0, ROPE), w80r[:, :, 0:ROPE]), (slice(64, 80), w80r[:, :, ROPE:])]
                    for a in range(2):
                        for h in range(2):
                            lo = ROPE + 16 * a + 8 * h
                            parts.append((slice(lo, lo + 8), kr[:, :, a, 1 - h]))
                    for cols, raw in parts:
                        dve.tensor_tensor(w80l[:, :, cols], raw, w80h[:, :, cols].bitcast(F32), ALU.subtract).then_inc(s_80lo, 1)
                    return
                dve.wait_ge(s_whi, w + 1 + 4 * j)
                dve.tensor_tensor(wlo[:, w % 2], wraw[:, (w // 2) % 2, :, (w % 2) * P:(w % 2 + 1) * P],
                                  whi[:, w % 2].bitcast(F32), ALU.subtract).then_inc(s_wlo, 1)

            def norm(n):
                if n not in sums or not sums[n][4]:
                    return
                what, kind, i = sums[n][:3]
                dve.wait_ge(s_rs, 2 * n_norms(n))
                lat = slice(0, T)
                if kind in ("cq", "ckv"):
                    dst, g0, tiles = (qT, V_GQ, 4) if kind == "cq" else (kT, V_GKV, 2)
                    tok, src = (slice(T, TA), rs[:, 0:TC]) if what == "ckvc" else (lat, rs[:, 0:T])
                    ops = [(dst[:, t, tok], vecs[:, g0 + t:g0 + t + 1], dst[:, t, tok], src) for t in range(tiles)]
                elif what == "kc":
                    ops = [(kT[:, :, T:], 1.0, kT[:, :, T:], rs[:, 0:T].rearrange("p (h n) -> p h n", h=DH))]
                else:
                    dst = qT if kind == "q" else kT
                    ops = [(dst[:, i, lat], DK ** -0.5 if kind == "q" else 1.0, dst[:, i, lat], rs[:, 0:T])]
                for m, (o, g, a, b) in enumerate(ops):
                    ins = dve.scalar_tensor_tensor(out=o, in0=a, scalar=g, in1=b, op0=ALU.mult, op1=ALU.mult)
                    if m == len(ops) - 1:
                        ins.then_inc(s_nrm, 1)

            def conv(n):
                kind, i = steps[n]
                base = 3 * (n % 2)
                if kind == "b":
                    dve.wait_ge(s_mm, n + 1)
                    own.mark(dve.tensor_tensor(cy[0:ROPE, 0:T], two(base)[ROPE:64], rope[ROPE:64], ALU.mult))
                    own.mark(dve.tensor_tensor(krf[:, 0:T], two(base)[0:ROPE], rope[0:ROPE], ALU.mult))
                    own.wait()
                    dve.tensor_tensor(krf[:, 0:T], krf[:, 0:T], cy[0:ROPE, 0:T], ALU.add).then_inc(s_kr, 1)
                if not is_conv(kind):
                    return
                m, col = n_conv(n), n_conv(n)
                w = T if kind == "q" else TA + 2
                dve.wait_ge(s_ev, n + 1)
                if kind != "q":
                    dve.wait_ge(s_rawc, m - 3)
                if m:
                    dve.wait_ge(s_sil, m)
                else:
                    dve.wait_ge(s_kr, 1)
                src = craw[:, m % 2]
                own.mark(dve.tensor_scalar(cy[:, 0:w], src[:, 0:w], vecs[:, V_CONV + 0 * 3 * DH + m:V_CONV + 0 * 3 * DH + m + 1], None, ALU.mult))
                own.wait()
                own.mark(dve.scalar_tensor_tensor(out=cy[:, 0:w], in0=src[:, 1:w + 1], scalar=vecs[:, V_CONV + 1 * 3 * DH + m:V_CONV + 1 * 3 * DH + m + 1],
                                                  in1=cy[:, 0:w], op0=ALU.mult, op1=ALU.add))
                own.wait()
                dve.scalar_tensor_tensor(out=cy[:, 0:w], in0=src[:, 2:w + 2], scalar=vecs[:, V_CONV + 2 * 3 * DH + m:V_CONV + 2 * 3 * DH + m + 1],
                                         in1=cy[:, 0:w], op0=ALU.mult, op1=ALU.add).then_inc(s_conv, 1)

            split_lo(0)
            for n in range(G0 + 2):
                split_lo(n + 1)
                norm(n - 1)
                if n:
                    conv(n - 1)
            with dve.Fori(0, 3) as j:
                for n in range(G0 + 2, G0 + 6):
                    split_lo(n + 1, j)
            split_lo(G0 + 15)

            after_projection(dve)
            dve.wait_ge(s_baT, 1)
            dve.wait_ge(s_lv, 48)
            a_t = ps[:, 0, 0:NA * 16].rearrange("p (t n) -> p t n", t=NA)[:, :, 8:16]
            dve.wait_ge(s_beta, 1)
            own.mark(dve.tensor_tensor(gtmp[:, 0], a_t, dtb[:].unsqueeze(1).broadcast_to([P, NA, 8]), ALU.add))
            own.wait()
            own.mark(dve.tensor_scalar(gtmp[:, 1], gtmp[:, 0], 0.0, None, ALU.max))
            own.wait()
            dve.scalar_tensor_tensor(out=gtmp[:, 2], in0=gtmp[:, 1], scalar=-2.0, in1=gtmp[:, 0],
                                     op0=ALU.mult, op1=ALU.add).then_inc(s_g, 1)
            dve.wait_ge(s_beta, 2)
            own.mark(dve.tensor_tensor(gtmp[:, 1], gtmp[:, 1], gtmp[:, 2], ALU.add))
            own.wait()
            dve.scalar_tensor_tensor(out=gg[:], in0=gtmp[:, 1], scalar=-1.0,
                                     in1=alog[:].unsqueeze(1).broadcast_to([P, NA, 8]), op0=ALU.mult, op1=ALU.mult).then_inc(s_g, 1)
            dve.wait_ge(s_beta, 3)
            dve.tensor_scalar(negeg[:], egs[:, 0], -1.0, None, ALU.mult).then_inc(s_g, 1)
            for what, s, d, k in schedule():
                if what == "mod":
                    continue
                key = (what, s, d, k)
                t = tile_at[d][s]
                if what == "prep" and k == 1:
                    b = full(dve, (*key, "KK"))
                    dve.wait_ge(s_decb, nth(d, s + 1))
                    if s:
                        dve.wait_ge(s_e1, nth(d, s))
                    dve.tensor_tensor(U[:, d, 0], heads(b), decb[:, d, 0], ALU.mult).then_inc(s_U, 1)
                    if s >= NC:
                        b = full(dve, (*key, "KQ"))
                        dve.tensor_tensor(QK[:, d, s % 2], heads(b), dec[:, d, 0], ALU.mult).then_inc(s_QK, 1)
                elif what == "prep" and k == 2:
                    dve.wait_ge(s_e1, nth(d, s + 1))
                    if s >= 2:
                        full(dve, ("scan", s - 2, d, 2, "X"))
                    dve.tensor_tensor(V[:, d, s % 2], per_column(ident), e1[:, d, 0], ALU.subtract).then_inc(s_V, 1)
                elif what == "prep" and k >= 3 and k % 3 == 0:
                    b = full(dve, (*key, "W"))
                    dve.tensor_tensor(Wt[:, d, 0], heads(b), per_column(levels[:, d, k // 3]), ALU.mult).then_inc(s_Wt, 1)
                elif what == "prep" and k >= 3 and k % 3 == 1:
                    b = full(dve, (*key, "H"))
                    dve.wait_ge(s_V, nth(d, (NL + 1) * s + k // 3))
                    dve.tensor_tensor(V[:, d, s % 2], V[:, d, s % 2], heads(b), ALU.subtract).then_inc(s_V, 1)
                elif what == "scan" and k == 0:
                    b = full(dve, (*key, "kT"))
                    dve.tensor_tensor(ks[:, d, 0], heads(b), per_head(egs[:, 1, d, t]), ALU.mult).then_inc(s_ks, 1)
                elif what == "scan" and k == 1:
                    dve.wait_ge(s_vt, nth(d, s + 1))
                    if s:
                        b = full(dve, (*key, "KS"))
                        if s > 1:
                            dve.wait_ge(s_r, nth(d, s))
                        dve.tensor_tensor(r1[:, d, 0], heads(b), per_head(negeg[:, d, t]), ALU.mult).then_inc(s_r1, 1)
                        dve.wait_ge(s_r1, nth(d, s))
                        dve.tensor_tensor(rr[:, d, 0], r1[:, d, 0], vt[:, d, 0], ALU.add).then_inc(s_r, 1)
                    else:
                        dve.tensor_copy(rr[:, d, 0], vt[:, d, 0]).then_inc(s_r, 1)
                elif what == "scan" and k == 2:
                    b = full(dve, (*key, "X"))
                    dve.tensor_tensor(vn[:, d, 0], heads(b), per_head(beta[:, t, 4 * d:4 * d + 4]), ALU.mult).then_inc(s_vn, 1)
                elif what == "scan" and k == 3:
                    b = full(dve, (*key, "SU"))
                    if s:
                        dve.wait_ge(s_Sg, nth(d, s))
                        dve.tensor_tensor(S[:, d, 0], heads(b), Sg[:, d, 0], ALU.add).then_inc(s_S, 1)
                    else:
                        dve.tensor_copy(S[:, d, 0], heads(b)).then_inc(s_S, 1)
                    if s >= NC + 4:
                        b = full(dve, (*key, "O"))
                        dve.wait_ge(s_oc, 8)
                        o = oT[:, :, t * P:(t + 1) * P]
                        dve.tensor_tensor(o, heads(b), o, ALU.add).then_inc(s_oa, 1)

            dve.wait_ge(s_m2, 2 * M2)
            m2 = ps[:, 7, 0:8 * KD].rearrange("p (k a) -> p k a", a=2)
            bias = vecs[:, V_BMOD + 2 * KD:V_BMOD + 6 * KD]
            own.mark(dve.tensor_tensor(gts[:, 0:KD], m2[:, 0:KD, 0], bias[:, 0:KD], ALU.add))
            own.mark(dve.tensor_tensor(modv[:, 2 * KD:], m2[:, KD:3 * KD], bias[:, KD:3 * KD].unsqueeze(2).broadcast_to([P, 2 * KD, 2]), ALU.add))
            dve.tensor_tensor(gts[:, KD:], m2[:, 3 * KD:, 0], bias[:, 3 * KD:], ALU.add).then_inc(s_grow, 1)
            own.wait()
            own.mark(dve.tensor_scalar(scale2[:], modv[:, 3 * KD:, 0], 1.0, None, ALU.add))
            own.wait()
            own.mark(dve.tensor_tensor(scale2[:], scale2[:], vecs[:, V_G2:V_G2 + KD], ALU.mult))
            own.wait()
            dve.wait_ge(s_gp, 32)
            dve.wait_ge(s_baT, 3)
            dve.tensor_tensor(gpost, ps[0:2 * KD, 7, 2 * P:3 * P], gpost, ALU.mult).then_inc(s_grow, 1)

            after_deltanet(dve)
            dve.wait_ge(s_hi, 1)
            dve.tensor_tensor(ckl[:], ck_raw, ckh[:].bitcast(F32), ALU.subtract).then_inc(s_lo, 1)
            dve.wait_ge(s_hi, 2)
            dve.tensor_tensor(uv_lo, uv_raw, uv_hi.bitcast(F32), ALU.subtract).then_inc(s_lo, 1)
            dve.wait_ge(s_z, 16)
            for h in range(DH):
                dve.wait_ge(s_grs, DH + h + 1)
                dve.scalar_tensor_tensor(out=oT[:, h], in0=oT[:, h], scalar=vecs[:, V_GDN:V_GDN + 1],
                                         in1=qT[:, h], op0=ALU.mult, op1=ALU.mult).then_inc(s_gnrm, 1)
                dve.wait_ge(s_gnrm, 2 * h + 1)
                dve.tensor_tensor(oT[:, h], oT[:, h], kT[:, h, 0:T], ALU.mult).then_inc(s_gnrm, 1)
                if h == 1:
                    for n in range(2):
                        dve.wait_ge(s_hi, n + 3)
                        dve.tensor_tensor(cql[:, 2 * n:2 * n + 2], cq_raw[n], cqh[:, 2 * n:2 * n + 2].bitcast(F32),
                                          ALU.subtract).then_inc(s_lo, 1)

            def rests_of_shared_key(p):
                for t0, tw in CH3:
                    own.mark(dve.tensor_copy(krl[:, 0:tw], kh[NOPE:QKD, p, t0:t0 + tw].bitcast(F32)))
                    own.wait()
                    own.mark(dve.tensor_tensor(kl[NOPE:QKD, p, t0:t0 + tw], krf[:, t0:t0 + tw], krl[:, 0:tw], ALU.subtract))
                    own.wait()

            def prepare(head, j, fills):
                p = head % 2
                for f in fills:
                    b, n = fill_at(head, f, j)
                    i = 5 * (head + 2 * j)
                    if f < F_K:
                        tok = slice(f * HALF, (f + 1) * HALF)
                        dve.wait_ge(s_pf[b], n)
                        if head or f:
                            dve.wait_ge(s_rp, 3 * (2 * (head + 2 * j) + f) - 2)
                        bank6 = ps[:, 6 + b, :]
                        dve.tensor_tensor(rot[NOPE:QKD, 0], bank6[NOPE:QKD], rope[NOPE:QKD, tok], ALU.mult)
                        dve.tensor_tensor(rot[NOPE:QKD, 1], bank6[QKD:P], rope[QKD:P, tok], ALU.mult).then_inc(s_rd, 1)
                        dve.wait_ge(s_qka, i + f + 1)
                        dve.tensor_tensor(ql[0:NOPE, p, tok], bank6[0:NOPE], qh[0:NOPE, p, tok].bitcast(F32),
                                          ALU.subtract).then_inc(s_pr[b], 1)
                    elif f < F_MAX:
                        t0, tw = CH3[f - F_K]
                        dve.wait_ge(s_pf[b], n)
                        dve.wait_ge(s_qka, i + f + 1)
                        dve.tensor_tensor(kl[0:NOPE, p, t0:t0 + tw], ps[0:NOPE, 6 + b, 0:tw],
                                          kh[0:NOPE, p, t0:t0 + tw].bitcast(F32), ALU.subtract).then_inc(s_pr[b], 1)
                    elif f < F_ROW:
                        qt, c = divmod(f - F_MAX, 3)
                        dve.wait_ge(s_pf[b], n)
                        if head and qt == 0 and c == 0:
                            dve.wait_ge(s_fin, head + 2 * j)
                        dve.tensor_reduce(mx[:, qt, c:c + 1], ps[:, 6 + b, 0:CH3[c][1]], AX.X, ALU.max).then_inc(s_pr[b], 1)
                        if f == F_ROW - 1:
                            dve.wait_ge(s_pr[b], n)
                            b1, n1 = fill_at(head, f - 1, j)
                            dve.wait_ge(s_pr[b1], n1)
                            dve.tensor_reduce(mpad[:, :, QKD], mx[:], AX.X, ALU.max).then_inc(s_fin, 1)
                            dve.wait_ge(s_fin, head + 1 + 2 * j)

            def one_head(head, j):
                for kt in range(NA):
                    if head < HEADS - 1:
                        prepare(head + 1, j, SLICES[kt])
                    n = NA * (head + 2 * j) + kt
                    dve.wait_ge(s_ex, n + 1)
                    dve.tensor_tensor(pl[:, kt % 2], pf[:], ph[:, kt % 2].bitcast(F32), ALU.subtract).then_inc(s_pl, 1)
                    if kt == 0 and head:
                        finish(head - 1, j)
                    if head == HEADS - 1 and kt == 5:
                        dve.wait_ge(s_mh, 1)
                        dve.tensor_tensor(odl[:], o_raw, odh[:].bitcast(F32), ALU.subtract).then_inc(s_ml, 1)
                    elif head == HEADS - 1 and kt in (7, 8):
                        stream_lo(kt - 7)

            def stream_lo(w, j=0, dst=None, hi=None):
                dve.wait_ge(s_wh, w + 1 + 4 * j)
                dve.tensor_tensor(wlo[:, w % 2] if dst is None else dst, wraw[:, w // 2 % 2, :, (w % 2) * P:(w % 2 + 1) * P],
                                  (whi[:, w % 2] if hi is None else hi).bitcast(F32), ALU.subtract).then_inc(s_wl, 1)

            def finish(head, j):
                dve.wait_ge(s_li, 2 * head + 2 + 4 * j)
                dve.tensor_tensor(ost[:], two(4)[0:VD], ost[:], ALU.mult).then_inc(s_on, 1)

            after_gating(dve)
            prepare(0, 0, range(F_MAX))
            dve.wait_ge(s_hi, 6)
            dve.wait_ge(s_init, 3)
            for p in range(2):
                rests_of_shared_key(p)
            prepare(0, 0, range(F_MAX, FILLS))
            heads_loop(dve, one_head)
            finish(HEADS - 1, 0)

            dve.wait_ge(s_mh, 2)
            dve.tensor_tensor(oal[:], a_raw, oah[:].bitcast(F32), ALU.subtract).then_inc(s_ml, 1)
            dve.wait_ge(s_ml, 2)
            def out_lo(c, tiles=range(4)):
                for i in tiles:
                    cols = slice(i * P, (i + 1) * P)
                    stream_lo(W_O + 4 * c + i, dst=wol[c][:, :, cols], hi=woh[c][:, :, cols])

            for m in range(KD):
                if m + 2 < W_O:
                    stream_lo(m + 2)
                else:
                    out_lo(0, (2 * (m % 2), 2 * (m % 2) + 1))
                dve.wait_ge(s_wm, m + 1)
                dve.wait_ge(s_gt[m % 2], 16 * (m // 2 + 1))
                for a in range(2):
                    g = gab[:, m % 2, a]
                    dve.tensor_tensor(g, two(4 * (m % 2) + 2 * a), g, ALU.mult).then_inc(s_mx, 1)
                dve.wait_ge(s_mx, 2 * m + 2)
                dve.tensor_tensor(merged[:, m], gab[:, m % 2, 0], gab[:, m % 2, 1], ALU.add).then_inc(s_mg, 1)
            def token_lo(t):
                dve.wait_ge(s_mth, t + 1)
                dve.tensor_tensor(mtl[:, t % 2], merged[:, :, t * P:(t + 1) * P], mth[:, t % 2].bitcast(F32),
                                  ALU.subtract).then_inc(s_mtl, 1)

            token_lo(0)
            out_lo(1)
            token_lo(1)
            feature = lambda a: a.unsqueeze(2).broadcast_to([P, KD, P])

            def modulate(t):
                dve.wait_ge(s_tr, t + 1)
                dst = merged[:, :, t * P:(t + 1) * P]
                own.mark(dve.tensor_tensor(dst, two(6).rearrange("p (k n) -> p k n", k=KD), feature(scale2[:]), ALU.mult))
                own.wait()
                dve.tensor_tensor(dst, dst, feature(modv[:, 2 * KD:3 * KD, 0]), ALU.add).then_inc(s_u2, 1)

            for t in range(NT):
                dve.wait_ge(s_ry, 2 * t + 2)
                own.mark(dve.reciprocal(orcp[:, 0, t:t + 1], oroot[:, 0, t:t + 1]))
                own.wait()
                if t == 0:
                    dve.wait_ge(s_G1, 16)
                else:
                    dve.wait_ge(s_res, t)
                dve.scalar_tensor_tensor(out=yt[:], in0=two(2 * (t % 3)), scalar=orcp[:, 0, t:t + 1], in1=G1[:],
                                         op0=ALU.mult, op1=ALU.mult).then_inc(s_y, 1)
                dve.wait_ge(s_y, t + 1)
                dve.wait_ge(s_xt[t % 2], XT0 + 16 * (t // 2 + 1))
                dve.tensor_tensor(xt[:, t % 2], xt[:, t % 2], yt[:], ALU.add).then_inc(s_res, 1)
                if t + 2 < NT:
                    token_lo(t + 2)
                dve.wait_ge(s_rx, 2 * t + 2)
                dve.reciprocal(orcp[:, 1, t:t + 1], oroot[:, 1, t:t + 1]).then_inc(s_rcx, 1)
                if t:
                    modulate(t - 1)
            modulate(NT - 1)
            stream_lo(W_FF)
            for c in range(2):
                for a, k0 in enumerate(range(0, KD, 2)):
                    at = (slice(None), slice(k0, k0 + 2), slice(c * HALF, (c + 1) * HALF))
                    dve.wait_ge(s_uh, 4 * c + a + 1)
                    dve.tensor_tensor(u2l[at], merged[at], u2h[at].bitcast(F32), ALU.subtract).then_inc(s_ul, 1)
                if c == 0:
                    stream_lo(W_FF + 1)
            for q in range(2):
                dve.wait_ge(s_s1[q], 16 * NT // 2)

            def hidden(i, j=0):
                if i + 1 < NFF:
                    stream_lo(W_FF + 2 * i + 2, j)
                dve.wait_ge(s_wm, KD + 2 * i + 2 + 2 * 2 * j)
                dve.wait_ge(s_sg, i + 1 + 2 * j)
                dve.tensor_tensor(hid[:, bass.ds(2 * j + i, 1)].rearrange("p a n -> p (a n)"), sg[:], two(4 * (i % 2) + 2),
                                  ALU.mult).then_inc(s_h, 1)
                if i + 1 < NFF:
                    stream_lo(W_FF + 2 * i + 3, j)
            hidden(0)
            with dve.Fori(0, NFF // 2 - 1) as j:
                hidden(1, j)
                hidden(2, j)
            hidden(NFF - 1)

            def rest_f2(half, k, j=0):
                m = NFF * half + k
                dve.wait_ge(s_gh, m + 1 + 2 * j)
                dve.tensor_tensor(wlo[:, m % 2, 0:4].rearrange("p a n -> p (a n)"), wraw[:, m % 2, 0:2].rearrange("p a n -> p (a n)"),
                                  whi[:, m % 2, 0:4].rearrange("p a n -> p (a n)").bitcast(F32), ALU.subtract)
                dve.tensor_tensor(hl[:, m % 2], hid[:, bass.ds(2 * j + k, 1)].rearrange("p a n -> p (a n)"),
                                  hh[:, m % 2].bitcast(F32), ALU.subtract).then_inc(s_gl, 1)
            for half in range(2):
                if half:
                    for t in range(NT):
                        dve.wait_ge(s_fq, t + 1)
                        dve.tensor_copy(f0[:, t], ps[:, t, :]).then_inc(s_f0, 1)
                rest_f2(half, 0)
                rest_f2(half, 1)
                with dve.Fori(0, NFF // 2 - 1) as j:
                    for k in (2, 3):
                        rest_f2(half, k, j)
            dve.wait_ge(s_G1, 32)
            dve.wait_ge(s_x1l, 16)
            dve.wait_ge(s_f0, NT)
            for t in range(NT):
                dve.wait_ge(s_fq, NT + t + 1)
                dve.tensor_tensor(osum[:, 3, t:t + 1], osum[:, 2, t:t + 1], osum[:, 3, t:t + 1], ALU.add).then_inc(s_fs, 1)
                dve.wait_ge(s_rf, t + 1)
                own.mark(dve.reciprocal(orcp[:, 2, t:t + 1], oroot[:, 2, t:t + 1]))
                own.wait()
                for half, src in enumerate((f0[:, t], ps[:, t, :])):
                    cols = slice(half * HALF, (half + 1) * HALF)
                    dve.scalar_tensor_tensor(out=hid[:, t, cols], in0=src, scalar=orcp[:, 2, t:t + 1], in1=G2[:, cols],
                                             op0=ALU.mult, op1=ALU.mult).then_inc(s_fy, 1)
                dve.wait_ge(s_fy, 3 * t + 2)
                dve.tensor_tensor(x1[:, t], x1[:, t], hid[:, t], ALU.add).then_inc(s_fy, 1)

        @block.tensor
        def _(pe):
            pe.wait_ge(s_const, 16 * 11)
            pe.transpose(ps[:, 7, 0:V_ROWS], vrow[:, :], tri[0:V_ROWS, 0, 0:V_ROWS]).then_inc(s_vT, 1)
            pe.wait_ge(s_silu, 2)
            for n in range(2 * MODP):
                pe.wait_ge(s_slot[n % 4], 16 * (n // 4 + 1))
                for k in range(KD):
                    mm = pe.matmul(ps[:, 0, 2 * n:2 * n + 2], slot_of(n)[:, k], scb[:, k, :],
                                   start=(k == 0), stop=(k == KD - 1))
                mm.then_inc(s_mod, 1)
            for n in range(24):
                g, k = divmod(n, KD)
                tiles = range(4 * g, min(4 * g + 4, NA))
                pe.wait_ge(s_xn, tiles[-1] + 1)
                if n >= 4:
                    pe.wait_ge(s_u, n - 3)
                for m in tiles:
                    mm = pe.transpose(ps[:, 1 + n % 4, (m % 4) * P:(m % 4 + 1) * P], xin[:, m, k * P:(k + 1) * P], ident)
                mm.then_inc(s_xT, 1)

            def sum_squares(n):
                if n not in sums:
                    return
                what, kind, i, start, stop = sums[n]
                if n_norms(n - 1):
                    pe.wait_ge(s_rs, 2 * n_norms(n - 1) - 1)
                if what == "lat":
                    pe.wait_ge(s_sq, n_sq(n))
                    for h in range(2):
                        mm = pe.matmul(ps[:, 6 + h, :], ones, sqb[:, h * HALF:(h + 1) * HALF], start=start, stop=stop)
                elif what == "ckvc":
                    pe.wait_ge(s_sqc, 2)
                    for h in range(2):
                        mm = pe.matmul(ps[:, 6, 0:TC], ones, sqc[h], start=(h == 0), stop=(h == 1))
                else:
                    pe.wait_ge(s_sqc, 6)
                    for h in range(2):
                        mm = pe.matmul(ps[:, 6 + h, :], ones, ys[:, 1, h * HALF:(h + 1) * HALF],
                                       start=True, stop=True)
                mm.then_inc(s_sum, 1)

            def products(n, j=0):
                kind, i = steps[n]
                w = tile_of.get(n)
                base = 3 * (n % 2)
                if w is None:
                    pe.wait_ge(s_80lo, 6)
                else:
                    pe.wait_ge(s_wlo, w + 1 + 4 * j)
                if n == 0:
                    pe.wait_ge(s_u, 24)
                    pe.wait_ge(s_modv, 1)
                if n >= 2:
                    pe.wait_ge(s_ev, n - 1 + 4 * j)
                if n == steps.index(("b", 0)) + 2:
                    pe.wait_ge(s_kr, 1)
                hi, lo, m = (w80h, w80l, 80) if w is None else (whi[:, w % 2], wlo[:, w % 2], P)
                for c, (t0, tw) in enumerate(chunks_of(kind)):
                    if n == 0:
                        pe.wait_ge(s_ulo, KD * (c + 1))
                    if n == 4 and c == 2:
                        pe.wait_ge(s_ulo, KD * 3)
                    for k in range(KD):
                        for a, b in ((hi, uhi), (hi, ulo), (lo, uhi)):
                            mm = pe.matmul(ps[0:m, base + c, 0:tw], a[:, k, :], b[:, k, t0:t0 + tw],
                                           start=(k == 0 and a is hi and b is uhi), stop=(k == KD - 1 and a is lo))
                mm.then_inc(s_mm, 1)

            for n in range(G0 + 2):
                products(n)
                sum_squares(n)
            with pe.Fori(0, 3) as j:
                for n in range(G0 + 2, G0 + 6):
                    products(n, j)
            products(G0 + 14)
            products(G0 + 15)

            after_projection(pe)
            pe.wait_ge(s_ba, 2)
            for t in range(NA):
                mm = pe.transpose(ps[:, 0, t * 16:(t + 1) * 16], ba[:, t * P:(t + 1) * P], tri[0:16, 0, 0:16])
            mm.then_inc(s_baT, 1)
            pe.wait_ge(s_g, 2)
            for a, tables in enumerate(((tLE, tGE), (tGT, tLT), (ones, ones))):
                for d in range(2):
                    at = (2 * a + d) * NA * DH
                    mm = pe.matmul(ps[:, 1, at:at + NA * DH].rearrange("p (t h) -> p t h", t=NA), tables[d],
                                   gg[:, :, 4 * d:4 * d + 4], start=True, stop=True)
            mm.then_inc(s_baT, 1)
            pe.wait_ge(s_beta, 3)

            def free(key):
                if last_fill[key]:
                    pe.wait_ge(*reader(*last_fill[key]))
                return fill[key][0]

            def four(key, ops, transpose=False):
                for h in range(DH):
                    for m, (a, b) in enumerate(ops(h)):
                        out = ps[:, fill[key][0], h * P:(h + 1) * P]
                        if transpose:
                            mm = pe.transpose(out, a, ident)
                        else:
                            mm = pe.matmul(out, a, b, start=(m == 0), stop=(m == len(ops(h)) - 1))
                mm.then_inc(s_full[fill[key][0]], 1)

            for what, s, d, k in schedule():
                key = (what, s, d, k)
                if what == "mod":
                    pe.wait_ge(s_m2p[s // 2 % 2], MP0 + 16 * (s // 4 + 1))
                    for kt in range(KD):
                        mm = pe.matmul(ps[:, 7, 2 * s:2 * s + 2], slot_of(s)[:, kt], scb[:, kt, :],
                                       start=(kt == 0), stop=(kt == KD - 1))
                    mm.then_inc(s_m2, 1)
                    continue
                t = tile_at[d][s]
                tok = slice(t * P, (t + 1) * P)
                names = [n for n, _ in fills_of(what, s, d, k)]
                for name in names:
                    b = free((*key, name))
                    to = (*key, name)
                    if name == "DEC":
                        pe.wait_ge(s_lg, nth(d, s + 1))
                        pe.matmul(ps[:, b, :], tGT if d == 0 else tLT, lg[:, d, 0].rearrange("p h n -> p (h n)"),
                                  start=True, stop=True).then_inc(s_full[b], 1)
                    elif name == "GC":
                        pe.matmul(ps[:, b, :], ones, lg[:, d, 0].rearrange("p h n -> p (h n)"),
                                  start=True, stop=True).then_inc(s_full[b], 1)
                    elif name == "KK":
                        four(to, lambda h: [(kT[:, h, tok], kT[:, h, tok])])
                    elif name == "KQ":
                        four(to, lambda h: [(kT[:, h, tok], qT[:, h, tok])])
                    elif name == "TR":
                        pe.wait_ge(s_V, nth(d, (NL + 1) * s + (1 if k == 2 else k // 3 + 1)))
                        four(to, lambda h: [(V[:, d, s % 2, h], None)], transpose=True)
                    elif name == "W":
                        pe.wait_ge(s_VT, nth(d, NL * s + k // 3))
                        four(to, lambda h: [(U[:, d, 0, h], VT[:, d, 0, h])])
                    elif name == "H":
                        pe.wait_ge(s_Wt, nth(d, NL * s + k // 3))
                        four(to, lambda h: [(Wt[:, d, 0, h], V[:, d, s % 2, h])])
                    elif name == "vT":
                        pe.wait_ge(s_vst[s % 2], 32 * (s // 2 + 1))
                        four(to, lambda h: [(vst[:, d, s % 2, h], None)], transpose=True)
                    elif name == "kT":
                        four(to, lambda h: [(kT[:, h, tok], None)], transpose=True)
                    elif name == "KS":
                        pe.wait_ge(s_S, nth(d, s))
                        four(to, lambda h: [(kT[:, h, tok], S[:, d, 0, h])])
                    elif name == "X":
                        pe.wait_ge(s_r, nth(d, s + 1))
                        pe.wait_ge(s_V, nth(d, (NL + 1) * (s + 1)))
                        four(to, lambda h: [(V[:, d, s % 2, h], rr[:, d, 0, h])])
                    elif name == "O":
                        pe.wait_ge(s_vn, nth(d, s + 1))
                        pe.wait_ge(s_qs, nth(d, s - NC + 1))
                        pe.wait_ge(s_QK, nth(d, s - NC + 1))
                        four(to, lambda h: [(S[:, d, 0, h], qs[:, d, s % 2, h]), (vn[:, d, 0, h], QK[:, d, s % 2, h])])
                    elif name == "SU":
                        pe.wait_ge(s_vn, nth(d, s + 1))
                        pe.wait_ge(s_ks, nth(d, s + 1))
                        four(to, lambda h: [(ks[:, d, 0, h], vn[:, d, 0, h])])

            pe.wait_ge(s_grow, 1)
            pe.transpose(ps[0:2 * KD, 7, 2 * P:3 * P], gts[:], ident).then_inc(s_baT, 1)

            after_deltanet(pe)
            for h in range(DH):
                pe.wait_ge(s_gsq, h + 1)
                if h == DH - 1:
                    pe.wait_ge(s_grow, 2)
                for c in range(2):
                    mm = pe.matmul(ps[:, 2 * h + c, :], ones, qT[:, h, c * HALF:(c + 1) * HALF], start=True, stop=True)
                mm.then_inc(s_gsm, 1)

            def three(out, pairs, k, start, stop):
                (ah, al), (bh, bl) = pairs
                pe.matmul(out, ah(k), bh(k), start=start, stop=False)
                pe.matmul(out, al(k), bh(k), start=False, stop=False)
                return pe.matmul(out, ah(k), bl(k), start=False, stop=stop)

            pe.wait_ge(s_grs, DH)
            pe.wait_ge(s_lo, 2)
            for t in range(NA):
                if t >= 4:
                    pe.wait_ge(s_vf, t - 3)
                tok = slice(t * P, (t + 1) * P)
                for k in range(CKV // P):
                    mm = three(ps[:, t % 4, :], ((lambda k: ckh[:, k, tok], lambda k: ckl[:, k, tok]),
                                                 (lambda k: uv_hi[:, k], lambda k: uv_lo[:, k])),
                               k, k == 0, k == CKV // P - 1)
                mm.then_inc(s_vp, 1)

            def prepare(head, j, fills):
                p = head % 2
                for f in fills:
                    b, n = fill_at(head, f, j)
                    if f == 0:
                        pe.wait_ge(s_aw, AW * (head + 1 + 2 * j))
                        pe.wait_ge(s_lo, 4)
                    if head or f >= 2:
                        pe.wait_ge(s_pr[b], n - 1)
                    out = ps[:, 6 + b, :]
                    if f < F_K:
                        tok = slice(f * HALF, (f + 1) * HALF)
                        for k in range(CQ // P):
                            mm = three(out, ((lambda k: whi[:, p, k], lambda k: wlo[:, p, k]),
                                             (lambda k: cqh[:, k, tok], lambda k: cql[:, k, tok])), k, k == 0, k == CQ // P - 1)
                    elif f < F_MAX:
                        t0, tw = CH3[f - F_K]
                        wk = [w[:, p, 4].rearrange("p (k n) -> p k n", k=CKV // P) for w in (whi, wlo)]
                        for k in range(CKV // P):
                            mm = three(out[0:NOPE, 0:tw], ((lambda k: wk[0][:, k], lambda k: wk[1][:, k]),
                                                           (lambda k: ckh[:, k, t0:t0 + tw], lambda k: ckl[:, k, t0:t0 + tw])),
                                       k, k == 0, k == CKV // P - 1)
                    elif f < F_ROW:
                        qt, c = divmod(f - F_MAX, 3)
                        if f == F_MAX:
                            pe.wait_ge(s_qka, 5 * (head + 1 + 2 * j))
                            pe.wait_ge(s_rp, 6 * (head + 1 + 2 * j))
                        t0, tw = CH3[c]
                        mm = pe.matmul(out[:, 0:tw], qh[0:QKD, p, qt * P:(qt + 1) * P], kh[0:QKD, p, t0:t0 + tw],
                                       start=True, stop=True)
                    else:
                        pe.wait_ge(s_fin, head + 1 + 2 * j)
                        for q in range(4):
                            mm = pe.transpose(out[0:QKD + 1, q * P:(q + 1) * P], mpad[:, 4 * (f - F_ROW) + q, :], ident)
                    mm.then_inc(s_pf[b], 1)

            def values(head, j, kt, between=()):
                n = NA * (head + 2 * j) + kt
                p = head % 2
                pe.wait_ge(s_pl, n + 1)
                if kt == 0:
                    pe.wait_ge(s_av, 2 * (head + 1 + 2 * j))
                    if head:
                        pe.wait_ge(s_on, head + 2 * j)
                for c in range(2):
                    if c:
                        prepare(head + 1, j, between)
                    tok = slice(c * HALF, (c + 1) * HALF)
                    pe.matmul(ps[:, 4 + c, :], vh[:, p, kt], ph[:, kt % 2, tok], start=(kt == 0), stop=False)
                    pe.matmul(ps[0:VD, 4 + c, :], vl[:, p, kt], ph[:, kt % 2, tok], start=False, stop=False)
                    mm = pe.matmul(ps[:, 4 + c, :], vh[:, p, kt], pl[:, kt % 2, tok], start=False, stop=(kt == NA - 1))
                mm.then_inc(s_pv, 1)

            def one_head(head, j):
                p = head % 2
                for kt in range(NA):
                    n = NA * (head + 2 * j) + kt
                    if kt == 0:
                        for b in range(2):
                            last = [f for f in range(FILLS) if fill_at(head, f, 0)[0] == b][-1]
                            pe.wait_ge(s_pr[b], fill_at(head, last, j)[1])
                    if head or kt >= 2:
                        pe.wait_ge(s_ex, n - 1)
                    keys = slice(kt * P, (kt + 1) * P)
                    ahead = PLACES[3 * kt:3 * kt + 3] if head < HEADS - 1 else [(), (), ()]
                    for c in range(2):
                        tok = slice(c * HALF, (c + 1) * HALF)
                        out = ps[:, 2 * (kt % 2) + c, :]
                        pe.matmul(out, kh[:, p, keys], qh[:, p, tok], start=True, stop=False)
                        pe.matmul(out, kl[:, p, keys], qh[0:QKD, p, tok], start=False, stop=False)
                        mm = pe.matmul(out, kh[0:QKD, p, keys], ql[:, p, tok], start=False, stop=True)
                        if c:
                            mm.then_inc(s_sf, 1)
                        prepare(head + 1, j, ahead[c])
                    if kt:
                        values(head, j, kt - 1, ahead[2] if kt < NA - 1 else ())
                    else:
                        prepare(head + 1, j, ahead[2])
                if head < HEADS - 1:
                    prepare(head + 1, j, PLACES[3 * NA - 1])
                values(head, j, NA - 1)

            pe.wait_ge(s_vf, NA)
            prepare(0, 0, range(F_MAX))
            pe.wait_ge(s_init, 3)
            pe.wait_ge(s_hi, 6)
            prepare(0, 0, range(F_MAX, FILLS))
            heads_loop(pe, one_head)

            def branch(m, a):
                if a and m == 0:
                    pe.wait_ge(s_ex, NA * HEADS)
                    pe.wait_ge(s_ml, 1)
                if a:
                    pe.wait_ge(s_wl, m + 1)
                    if m >= 2:
                        pe.wait_ge(s_mg, m - 1)
                hi, lo, k0 = (odh, odl, DH) if a else (oah, oal, 0)
                for c in range(2):
                    tok = slice(c * HALF, (c + 1) * HALF)
                    for k in range(DH):
                        mm = three(ps[:, 4 * (m % 2) + 2 * a + c, :],
                                   ((lambda k: whi[:, m % 2, k0 + k], lambda k: wlo[:, m % 2, k0 + k]),
                                    (lambda k: hi[:, k, tok], lambda k: lo[:, k, tok])), k, k == 0, k == DH - 1)
                return mm

            branch(0, 1)
            branch(1, 1)
            pe.wait_ge(s_ml, 2)
            branch(0, 0).then_inc(s_wm, 1)
            branch(1, 0).then_inc(s_wm, 1)
            for m in range(2, KD):
                branch(m, 1)
                branch(m, 0).then_inc(s_wm, 1)

            def turn(t):
                pe.wait_ge(s_xnt, t + 1)
                if t:
                    pe.wait_ge(s_u2, t)
                for k in range(KD):
                    mm = pe.transpose(ps[:, 6 + k // 4, (k % 4) * P:(k % 4 + 1) * P], xn[:, k * P:(k + 1) * P], ident)
                mm.then_inc(s_tr, 1)

            for t in range(NT):
                pe.wait_ge(s_mtl, t + 1)
                if t >= 3:
                    pe.wait_ge(s_y, t - 2)
                for c in range(2):
                    if t == 0:
                        pe.wait_ge(s_wl, W_O + 4 * c + 4)
                    for k in range(KD):
                        mm = three(ps[:, 2 * (t % 3) + c, :], ((lambda k: mth[:, t % 2, k], lambda k: mtl[:, t % 2, k]),
                                                               (lambda k: woh[c][:, k], lambda k: wol[c][:, k])),
                                   k, k == 0, k == KD - 1)
                mm.then_inc(s_o, 1)
                if t >= 2:
                    turn(t - 2)
            turn(NT - 2)
            turn(NT - 1)

            def ffn(i, j=0, peeled=False):
                for a in range(2):
                    w = 2 * i + a
                    pe.wait_ge(s_wl, W_FF + w + 1 + 4 * j)
                    if a == 0 and i >= 2:
                        pe.wait_ge(s_h, i - 1 + 2 * j)
                    for c in range(2):
                        tok = slice(c * HALF, (c + 1) * HALF)
                        for k in range(KD):
                            if peeled and a == 0:
                                pe.wait_ge(s_ul, 4 * c + k // 2 + 1)
                            mm = three(ps[:, 4 * (i % 2) + 2 * a + c, :], ((lambda k: whi[:, a, k], lambda k: wlo[:, a, k]),
                                                                           (lambda k: u2h[:, k, tok], lambda k: u2l[:, k, tok])),
                                       k, k == 0, k == KD - 1)
                    mm.then_inc(s_wm, 1)
            ffn(0, peeled=True)
            ffn(1)
            with pe.Fori(0, NFF // 2 - 1) as j:
                ffn(2, j)
                ffn(3, j)

            def f2_products(half, k, t):
                m = NFF * half + k
                w = [a[:, m % 2, 0:4].rearrange("p a n -> p (a n)") for a in (whi, wlo)]
                tok = slice(t * P, (t + 1) * P)
                pe.matmul(ps[:, t, :], hh[:, m % 2, tok], w[0], start=(k == 0), stop=False)
                pe.matmul(ps[:, t, :], hh[:, m % 2, tok], w[1], start=False, stop=False)
                return pe.matmul(ps[:, t, :], hl[:, m % 2, tok], w[0], start=False, stop=(k == NFF - 1))

            def f2_step(half, k, j=0):
                m = NFF * half + k
                pe.wait_ge(s_gl, m + 1 + 2 * j)
                for t in range(NT):
                    if k == 0 and half == 0 and t == 0:
                        pe.wait_ge(s_h, NFF)
                    if k == 0 and half:
                        pe.wait_ge(s_f0, t + 1)
                    mm = f2_products(half, k, t)
                mm.then_inc(s_fm, 1)
            for half in range(2):
                f2_step(half, 0)
                f2_step(half, 1)
                with pe.Fori(0, NFF // 2 - 2) as j:
                    f2_step(half, 2, j)
                    f2_step(half, 3, j)
                pe.wait_ge(s_gl, NFF * (half + 1))
                for t in range(NT):
                    for k in (NFF - 2, NFF - 1):
                        mm = f2_products(half, k, t)
                    mm.then_inc(s_ft, 1)


_INS = ['x', 'c', 'ctx', 'c_ctx', 'w_mod', 'b_mod', 'g_pre_mix', 'g_post_mix', 'g_pre_ffn', 'g_post_ffn', 'w_in', 'g_q_lora', 'w_uq', 'g_kv_lora', 'w_ukv', 'w_o_mla', 'conv_qkv', 'a_log', 'dt_bias', 'g_dn_out', 'w_o_dn', 'w_out', 'w_ffn_in', 'w_ffn_out']
_OUTS = [((1, 1024, 1024), 'float32')]


def kernel(**inputs):
    import numpy as _np
    import concourse.bacc as _bacc
    from concourse import mybir as _mybir
    from concourse.bass_utils import run_bass_kernel_spmd as _run

    nc = _bacc.Bacc("TRN2", target_bir_lowering=False, num_devices=1)
    arrays, args = {}, []
    for name in _INS:
        a = _np.ascontiguousarray(inputs[name])
        arrays[f"in_{name}_dram"] = a
        args.append(nc.dram_tensor(f"in_{name}_dram", a.shape, _mybir.dt.from_np(a.dtype), kind="ExternalInput").ap())
    for name, a in zip(("tri", "levels", "rope"), constants()):
        arrays[f"in_{name}_dram"] = a
        args.append(nc.dram_tensor(f"in_{name}_dram", a.shape, _mybir.dt.from_np(a.dtype), kind="ExternalInput").ap())
    for i, (shape, dtype) in enumerate(_OUTS):
        dt = _mybir.dt.from_np(_np.dtype(dtype))
        args.append(nc.dram_tensor(f"out_{i}_dram", shape, dt, kind="ExternalOutput").ap())
    hybrid_mla_gdn_flow_block(nc, *args)
    r = _run(nc, [arrays], core_ids=[0])
    return r.results[0]["out_0_dram"]
```
